# Optimizing a Trainium2 kernel written in Bass

```python
import jax, jax.numpy as jnp
from jax import lax
import numpy as np

D_MODEL = 1024
BATCH = 1
SEQ = 256
DEPTH = 2
DEC_BATCH = 1
DEC_SEQ = 1024
PAST_LEN = 256

GRID_W = 64
N_EVEN = (DEPTH + 1) // 2
N_ODD = DEPTH // 2
A_WIDTH = D_MODEL // 2
A_GROUPS = 4
A_GROUP_DIM = A_WIDTH // A_GROUPS
CHUNK = 128
B_HEADS = 4
B_DK = (D_MODEL // 2) // B_HEADS
B_DV = (D_MODEL // 2) // B_HEADS
RET_CHUNK = 128
ROPE_BASE = 10000.0
ROPE_PAIRS_AXIS = B_DK // 4
POOL_WINDOWS = (2, 4, 8, 16)
POOL_GROUPS = len(POOL_WINDOWS)
POOL_DIM = D_MODEL // POOL_GROUPS
D_FF = 4 * D_MODEL
EPS = 1e-6
QK_W = B_HEADS * B_DK
V_W = B_HEADS * B_DV
IN_SPLITS = (A_WIDTH, 2 * A_WIDTH, 2 * A_WIDTH + QK_W, 2 * A_WIDTH + 2 * QK_W,
             2 * A_WIDTH + 2 * QK_W + V_W, 2 * A_WIDTH + 2 * QK_W + 2 * V_W)
IN_WIDTH = 2 * A_WIDTH + 2 * QK_W + 3 * V_W
OUT_WIDTH = A_WIDTH + V_W

kernel_name = "hybrid_gmlp_retention_pool_diffusion_step"

def _rms_norm(x, gain):
    xf = x.astype(jnp.float32)
    y = xf * lax.rsqrt(jnp.mean(xf * xf, axis=-1, keepdims=True) + EPS)
    return (y * gain.astype(jnp.float32)).astype(x.dtype)

def _layer_norm(x):
    xf = x.astype(jnp.float32)
    mu = jnp.mean(xf, axis=-1, keepdims=True)
    var = jnp.mean(jnp.square(xf - mu), axis=-1, keepdims=True)
    return (xf - mu) * lax.rsqrt(var + EPS)

def _rope_tables(n_tokens):
    rows = n_tokens // GRID_W
    pos_r = jnp.repeat(jnp.arange(rows, dtype=jnp.float32), GRID_W)
    pos_c = jnp.tile(jnp.arange(GRID_W, dtype=jnp.float32), rows)
    inv = ROPE_BASE ** (-jnp.arange(ROPE_PAIRS_AXIS, dtype=jnp.float32) / ROPE_PAIRS_AXIS)
    ang = jnp.concatenate([pos_r[:, None] * inv, pos_c[:, None] * inv], axis=-1)
    return jnp.cos(ang), jnp.sin(ang)

def _apply_rope(x, cos, sin):
    half = B_DK // 2
    x1, x2 = x[..., :half], x[..., half:]
    return jnp.concatenate([x1 * cos - x2 * sin, x1 * sin + x2 * cos], axis=-1)

def _chunk_gmlp(u, v, w_s, b_s, vnorm_gain):
    bsz, length, _ = u.shape
    n = length // CHUNK
    ug = u.reshape(bsz, n, CHUNK, A_GROUPS, A_GROUP_DIM)
    vg = _layer_norm(v.reshape(bsz, n, CHUNK, A_GROUPS, A_GROUP_DIM)).astype(u.dtype) * vnorm_gain
    sp = jnp.einsum('gij,bnjgc->bnigc', w_s, vg) + b_s.T[:, :, None]
    return (ug * sp).reshape(bsz, length, A_WIDTH)

def _retention_dir(q, k, v, log_gamma, s0):
    bsz, nh, length, dk = q.shape
    n = length // RET_CHUNK
    qc = q.reshape(bsz, nh, n, RET_CHUNK, dk)
    kc = k.reshape(bsz, nh, n, RET_CHUNK, dk)
    vc = v.reshape(bsz, nh, n, RET_CHUNK, B_DV)
    idx = jnp.arange(RET_CHUNK, dtype=jnp.float32)
    diff = idx[:, None] - idx[None, :]
    mask = diff >= 0
    decay = jnp.where(mask, jnp.exp(log_gamma[:, None, None] * jnp.where(mask, diff, 0.0)), 0.0)
    scores = jnp.einsum('bhnid,bhnjd->bhnij', qc, kc) * decay[None, :, None]
    y_inner = jnp.einsum('bhnij,bhnje->bhnie', scores, vc)
    q_decay = jnp.exp(log_gamma[:, None] * (idx + 1.0))
    k_decay = jnp.exp(log_gamma[:, None] * (RET_CHUNK - 1.0 - idx))
    chunk_decay = jnp.exp(log_gamma * RET_CHUNK)[None, :, None, None]
    kv = jnp.einsum('bhnjd,hj,bhnje->nbhde', kc, k_decay, vc)

    def step(s, kv_c):
        return chunk_decay * s + kv_c, s

    s_final, s_prev = lax.scan(step, s0.astype(jnp.float32), kv)
    y_cross = jnp.einsum('bhnid,hi,nbhde->bhnie', qc, q_decay, s_prev)
    return (y_inner + y_cross).reshape(bsz, nh, length, B_DV), s_final

def _retention_bidir(q, k, v, decay_param, s0):
    log_g = -jnp.exp(decay_param.astype(jnp.float32))
    y_f, s_f = _retention_dir(q, k, v, log_g[0], s0[:, 0])
    y_b, s_b = _retention_dir(q[:, :, ::-1], k[:, :, ::-1], v[:, :, ::-1], log_g[1], s0[:, 1])
    return y_f, y_b[:, :, ::-1], jnp.stack([s_f, s_b], axis=1)

def _even_mixer(h, rope, s0, w_in, w_s, b_s, vnorm_gain, decay_param, w_out):
    bsz, length, _ = h.shape
    z = h @ w_in
    u, v, q, k, val, g_f, g_b = jnp.split(z, IN_SPLITS, axis=-1)
    a_out = _chunk_gmlp(jax.nn.gelu(u), jax.nn.gelu(v), w_s, b_s, vnorm_gain)

    def heads(t, d):
        return t.reshape(bsz, length, B_HEADS, d).transpose(0, 2, 1, 3).astype(jnp.float32)

    qh = heads(q, B_DK)
    kh = heads(k, B_DK) * (B_DK ** -0.5)
    if rope is not None:
        cos, sin = rope
        qh = _apply_rope(qh, cos, sin)
        kh = _apply_rope(kh, cos, sin)
    y_f, y_b, s_new = _retention_bidir(qh, kh, heads(val, B_DV), decay_param, s0)

    def merge(y):
        return _layer_norm(y).transpose(0, 2, 1, 3).reshape(bsz, length, V_W).astype(h.dtype)

    b_out = jax.nn.silu(g_f) * merge(y_f) + jax.nn.silu(g_b) * merge(y_b)
    return jnp.concatenate([a_out, b_out], axis=-1) @ w_out, s_new

def _pool_mixer(h, w_pool, pool_scale):
    bsz, length, _ = h.shape
    hg = h.reshape(bsz, length, POOL_GROUPS, POOL_DIM).astype(jnp.float32)
    csum = jnp.concatenate([jnp.zeros((bsz, 1, POOL_GROUPS, POOL_DIM), jnp.float32),
                            jnp.cumsum(hg, axis=1)], axis=1)
    t = jnp.arange(length)
    outs = []
    for g, w in enumerate(POOL_WINDOWS):
        lo = jnp.clip(t - w // 2, 0, length)
        hi = jnp.clip(t + w // 2, 0, length)
        mean = (csum[:, hi, g] - csum[:, lo, g]) / (hi - lo).astype(jnp.float32)[None, :, None]
        outs.append(mean - hg[:, :, g])
    pooled = jnp.stack(outs, axis=2).astype(h.dtype)
    y = jnp.einsum('blgc,gcd->blgd', pooled, w_pool).reshape(bsz, length, D_MODEL)
    return y * pool_scale

def _trunk(x, cond, rope, s_init, ada_w, ada_b, norm_mix, norm_mlp, mlp_w1, mlp_w2,
           ev_w_in, ev_w_s, ev_b_s, ev_vnorm, ev_decay, ev_w_out, od_w_pool, od_pool_scale, final_norm):
    states = []
    for i in range(DEPTH):
        mod = (jax.nn.silu(cond) @ ada_w[i] + ada_b[i])[:, None, :]
        sh1, sc1, g1, sh2, sc2, g2 = jnp.split(mod, 6, axis=-1)
        h = _rms_norm(x, norm_mix[i]) * (1.0 + sc1) + sh1
        if i % 2 == 0:
            e = i // 2
            out, s_new = _even_mixer(h, rope, s_init[:, e], ev_w_in[e], ev_w_s[e], ev_b_s[e],
                                     ev_vnorm[e], ev_decay[e], ev_w_out[e])
            states.append(s_new)
        else:
            o = i // 2
            out = _pool_mixer(h, od_w_pool[o], od_pool_scale[o])
        x = x + g1 * out
        h = _rms_norm(x, norm_mlp[i]) * (1.0 + sc2) + sh2
        x = x + g2 * (jnp.square(jax.nn.relu(h @ mlp_w1[i])) @ mlp_w2[i])
    return _rms_norm(x, final_norm), jnp.stack(states, axis=1)

def setup_inputs(seed: int = 0) -> dict:
    key = jax.random.key(seed)
    ks = jax.random.split(key, 24)
    f32 = jnp.float32
    nrm = lambda k, shape, s: jax.random.normal(k, shape, f32) * s
    gammas = 1.0 - 2.0 ** (-5.0 - jnp.arange(B_HEADS, dtype=f32))
    decay_base = jnp.log(-jnp.log(gammas))
    return {
        "x_prompt": nrm(ks[0], (BATCH, SEQ, D_MODEL), 1.0),
        "x_sample": nrm(ks[1], (DEC_BATCH, DEC_SEQ, D_MODEL), 1.0),
        "state_ret": nrm(ks[2], (DEC_BATCH, N_EVEN, 2, B_HEADS, B_DK, B_DV), 0.5),
        "c": nrm(ks[3], (DEC_BATCH, D_MODEL), 1.0),
        "c_ctx": nrm(ks[4], (D_MODEL,), 1.0),
        "ada_w": nrm(ks[5], (DEPTH, D_MODEL, 6 * D_MODEL), 0.5 * D_MODEL ** -0.5),
        "ada_b": nrm(ks[6], (DEPTH, 6 * D_MODEL), 0.01),
        "norm_mix": 1.0 + nrm(ks[7], (DEPTH, D_MODEL), 0.05),
        "norm_mlp": 1.0 + nrm(ks[8], (DEPTH, D_MODEL), 0.05),
        "mlp_w1": nrm(ks[9], (DEPTH, D_MODEL, D_FF), D_MODEL ** -0.5),
        "mlp_w2": nrm(ks[10], (DEPTH, D_FF, D_MODEL), D_FF ** -0.5),
        "ev_w_in": nrm(ks[11], (N_EVEN, D_MODEL, IN_WIDTH), D_MODEL ** -0.5),
        "ev_w_s": nrm(ks[12], (N_EVEN, A_GROUPS, CHUNK, CHUNK), CHUNK ** -0.5),
        "ev_b_s": 1.0 + nrm(ks[13], (N_EVEN, A_GROUPS, CHUNK), 0.1),
        "ev_vnorm": 1.0 + nrm(ks[14], (N_EVEN, A_GROUPS, A_GROUP_DIM), 0.05),
        "ev_decay": decay_base[None, None, :] + nrm(ks[15], (N_EVEN, 2, B_HEADS), 0.1),
        "ev_w_out": nrm(ks[16], (N_EVEN, OUT_WIDTH, D_MODEL), OUT_WIDTH ** -0.5),
        "od_w_pool": nrm(ks[17], (N_ODD, POOL_GROUPS, POOL_DIM, POOL_DIM), POOL_DIM ** -0.5),
        "od_pool_scale": 1.0 + nrm(ks[18], (N_ODD, D_MODEL), 0.1),
        "final_norm": 1.0 + nrm(ks[19], (D_MODEL,), 0.05),
    }

def reference(x_prompt, x_sample, state_ret, c, c_ctx, ada_w, ada_b, norm_mix, norm_mlp, mlp_w1, mlp_w2,
              ev_w_in, ev_w_s, ev_b_s, ev_vnorm, ev_decay, ev_w_out, od_w_pool, od_pool_scale, final_norm):
    weights = (ada_w, ada_b, norm_mix, norm_mlp, mlp_w1, mlp_w2, ev_w_in, ev_w_s, ev_b_s, ev_vnorm,
               ev_decay, ev_w_out, od_w_pool, od_pool_scale, final_norm)
    s_zero = jnp.zeros((x_prompt.shape[0], N_EVEN, 2, B_HEADS, B_DK, B_DV), jnp.float32)
    y_prompt, new_state_ret = _trunk(x_prompt, c_ctx[None, :], None, s_zero, *weights)
    rope = _rope_tables(x_sample.shape[1])
    y_sample, _ = _trunk(x_sample, c, rope, state_ret, *weights)
    return (y_prompt, y_sample, new_state_ret.astype(x_prompt.dtype))


_drawn_inputs = setup_inputs


def setup_inputs(seed=0):
    import zlib

    import numpy as np

    out = dict(_drawn_inputs(seed))
    spreads = {}
    factors = {'ev_b_s': 3.946,
     'ev_vnorm': 7.988,
     'state_ret': 2.749,
     'norm_mlp': 2.959,
     'od_pool_scale': 3.259}
    for name, (base, spread) in spreads.items():
        noise = np.random.default_rng([zlib.crc32(name.encode()), seed]).standard_normal(out[name].shape)
        drawn = base * np.exp(spread * noise) if base else spread * noise
        out[name] = __import__('jax').numpy.asarray(drawn.astype(out[name].dtype))
    for name, factor in factors.items():
        out[name] = (out[name] * factor).astype(out[name].dtype)
    return out
```

```python
import numpy as np
import concourse.bass as bass
from concourse import mybir

F32 = mybir.dt.float32
F32R = mybir.dt.float32r
ALU = mybir.AluOpType
ACT = mybir.ActivationFunctionType

P = 128
D = 1024
DT = D // P
SAMPLE, PROMPT = 1024, 256
T = SAMPLE + PROMPT
NT = T // P
NS = SAMPLE // P
HEADS = 4
HW = HEADS * P
F = 4096
UC = 256
NCH = F // UC
HT = UC // P
NMOD = 6 * DT
EPS = 1e-6
WINDOWS = (2, 4, 8, 16)
PADW = 8
PW = SAMPLE + PROMPT + 4 * PADW
TB = [(0, 512, 1), (512, 512, 1), (1024, 256, 0)]
NTB = len(TB)
GRP = NTB * DT
GRID_W = 64

IN_UNITS = ([("v", i, 512 + i * UC, True) for i in range(2)] + [("u", i, i * UC, False) for i in range(2)]
            + [("q", i, 1024 + i * UC, False) for i in range(2)] + [("k", i, 1536 + i * UC, False) for i in range(2)]
            + [("val", i, 2048 + i * UC, True) for i in range(2)] + [("gf", i, 2560 + i * UC, True) for i in range(2)]
            + [("gb", i, 3072 + i * UC, True) for i in range(2)])
N_IN = len(IN_UNITS)
U_OUT = N_IN
N_OUT = D // UC
U_MLP = [U_OUT + N_OUT, U_OUT + N_OUT + 2 * NCH + 1]
U_POOL = U_MLP[1] - 1
IN_GROUPS = [NT if tok else NTB * HT for _, _, _, tok in IN_UNITS]
IN_CUM = [sum(IN_GROUPS[:i]) for i in range(N_IN + 1)]
ADA_IN = NMOD - 2 * DT
ADA_PER_CHUNK = NMOD // NCH

BY_BLOCK = [(t, d) for t in range(NTB) for d in range(DT)]
BY_PAIR = [(t, HT * u + f) for u in range(DT // HT) for t in range(NTB) for f in range(HT)]
NORM_ORDER = [BY_BLOCK, BY_PAIR, BY_BLOCK, BY_PAIR, BY_BLOCK]


def add_numbers(order):
    out, n = {}, 0
    for t, d in order:
        if d == 0:
            out[(t, d)] = None
        else:
            out[(t, d)] = n
            n += 1
    return out


ADDS = [add_numbers(o) for o in NORM_ORDER]
ADDS_PER_NORM = GRP - NTB

RSTEPS = [(s, NS - 1 - s) for s in range(NS - 1)] + [(NS, NS + 1), (NS + 1, NS)]


def after(eng, sem, n):
    if isinstance(n, int) and n <= 0:
        return
    eng.wait_ge(sem, n)


def build(nc, ctx, x_prompt, x_sample, state_ret, c, c_ctx, ada_w, ada_b, norm_mix, norm_mlp, mlp_w1, mlp_w2,
          ev_w_in, ev_w_s, ev_b_s, ev_vnorm, ev_decay, ev_w_out, od_w_pool, od_pool_scale, final_norm,
          small_const, pos_const, rope_const, y_prompt, y_sample, new_state):
    KB = 1024
    base = (nc.sbuf_base + 31) // 32 * 32

    def at(name, kb, shape, dt=F32):
        return nc.alloc_sbuf_tensor_at(name, shape, dt, offset=base + int(kb * KB))

    A_H, A_L, A_X, A_M, A_E, A_R0, A_R1, A_ST, A_AD, A_C = 0, 40, 80, 120, 140, 160, 176, 192, 200, 204
    hH = at("hH", A_H, [P, DT, T], F32R)
    hL = at("hL", A_L, [P, DT, T], F32R)
    X = at("X", A_X, [P, DT, T])
    midH = at("midH", A_M, [P, HT, T], F32R)
    midL = at("midL", A_M + 10, [P, HT, T], F32R)
    ringH = [at(f"ringH{i}", a, [P, 2048], F32R) for i, a in enumerate((A_R0, A_R1))]
    ringL = [at(f"ringL{i}", a + 8, [P, 2048], F32R) for i, a in enumerate((A_R0, A_R1))]
    stage = at("stage", A_ST, [P, 2048])
    ada_st = at("ada_st", A_AD, [P, DT, P])
    xn_b = [at(f"xn{i}", A_E + 2 * i, [P, 512]) for i in range(2)]
    hs_b = [at(f"hs{i}", A_E + 4 + 2 * i, [P, 512]) for i in range(2)]
    sq_b = [at(f"sq{i}", A_E + 11 + 2 * i, [P, 512]) for i in range(2)]
    xtok = at("xtok", A_H, [P, NT, D])
    ada0 = [at(f"ada0_{i}", a, [P, DT, UC]) for i, a in enumerate([A_L + 8 * j for j in range(5)]
                                                                   + [A_M, A_M + 8, A_R1])]
    rows = at("rows", A_R1 + 8, [P, P])
    ada_rows = at("ada_rows", A_R1 + 8.5, [P, P])
    vtok = at("vtok", A_M, [P, NT, 512])
    ug = [at(f"ug{i}", A_E + 2 * i, [P, 512]) for i in range(2)]
    ws_raw = at("ws_raw", A_E, [P, 4, P])
    ga = [at(f"ga{i}", A_E + 4 + 2 * i, [P, 512]) for i in range(2)]
    gaH = [at(f"gaH{i}", A_E + 8 + 2 * i, [P, 512], F32R) for i in range(2)]
    gaL = [at(f"gaL{i}", A_E + 12 + 2 * i, [P, 512], F32R) for i in range(2)]
    bias_b = at("bias_b", A_E + 16, [P, 4, P])
    wsT = at("wsT", A_E + 18, [P, 4, P])
    qk = at("qk", A_X, [P, 2 * HEADS, T])
    rope = at("rope", A_M, [P, 2, SAMPLE])
    swap = [at(f"swap{i}", A_M + 8 + 4 * i, [P, SAMPLE]) for i in range(2)]
    val = at("val", A_E, [P, NT, HW])
    gate_st = at("gate_st", A_M, [P, NT, UC])
    tab = at("tab", A_M + 10, [P, 4, HEADS, P])
    kx = [at(f"kx{i}", A_M + 4 * i, [P, 2, HEADS, P]) for i in range(2)]
    pt = [at(f"pt{i}", A_M + 4 * i, [P, 2, HEADS, P]) for i in range(2)]
    S = [at("SF", A_H, [P, NT, HEADS, P]), at("SB", A_L, [P, NT, HEADS, P])]
    qd = [at(f"qd{i}", A_R1 + 4 * i, [P, 2, HEADS, P]) for i in range(2)]
    yn = [at(f"yn{i}", A_R1 + 8 + 4 * i, [P, 2, HEADS, P]) for i in range(2)]
    new_st = at("new_st", A_R1 + 8, [P, 2, HEADS, P])
    gt = [at(f"gt{i}", A_ST + 4 * i, [P, 2, 2, UC]) for i in range(2)]
    prow = [[at(f"prow{i}_{j}", A_M + (3 * i + j) * PW * 4 / KB, [P, PW]) for j in range(3)] for i in range(2)]
    yT = at("yT", A_H, [P, DT, T])
    ytok = at("ytok", A_L, [P, NT, D])

    off = [A_C]

    def small(name, shape):
        n = int(np.prod(shape[1:])) * 4
        t = at(name, off[0], shape)
        off[0] += ((n + 31) // 32 * 32) / KB
        return t

    csm = small("csm", [P, P + 2 + 64])
    ident = csm[:, 0:P]
    edges = csm[:, P + 2:P + 66].rearrange("p (g s e) -> p g s e", g=4, s=2)
    vec = small("vec", [P, 68])
    adab = small("adab", [P, 2 * NMOD])
    sc2 = small("sc2", [P, DT, 2])
    mod = small("mod", [P, 2, NMOD, 2])
    gain = [small(f"gain{q}", [P, DT, 2]) for q in range(4)]
    gpool = small("gpool", [P, DT, 2])
    eps_t = small("eps_t", [P, 1])
    dec = small("dec", [P, 8])
    ned = small("ned", [P, 8])
    kd = small("kd", [P, 8])
    cd = small("cd", [P, 8])
    vmv = small("vmv", [P, NT * 4, 2])
    vst = small("vst", [P, NT * 4, 6])
    rst = [small(f"rst{i}", [P, 8, 6]) for i in range(2)]
    rmv = [small(f"rmv{i}", [P, 8, 2]) for i in range(2)]
    rnm = [small(f"rnm{i}", [P, 8]) for i in range(2)]
    ones = small("ones", [P, P])
    r_b = [small(f"relu{i}", [P, 512]) for i in range(3)]
    acc2 = [at("acc0", A_E + 15, [P, T]), small("acc1", [P, T])]
    assert base + off[0] * KB <= nc.sbuf_usable_end, (base + off[0] * KB, nc.sbuf_usable_end)

    bank = [nc.alloc_psum_tensor(f"bank{i}", [P, 512], F32) for i in range(8)]
    ADA_BANK, WS_BANK = bank[7], bank[6]

    x_dram = nc.dram_tensor("x_spill", [P, DT, T], F32, kind="Internal").ap()
    a_dram = nc.dram_tensor("a_spill", [2, P, HEADS, T], F32, kind="Internal").ap()
    g_dram = nc.dram_tensor("gate_spill", [4, P, NT, UC], F32, kind="Internal").ap()

    ada_v = [ada_w[l].rearrange("(k p) f -> p k f", p=P) for l in range(2)]
    win_v = ev_w_in[0].rearrange("(k p) f -> p k f", p=P)
    wout_v = ev_w_out[0].rearrange("(k p) f -> p k f", p=P)
    w1_v = [mlp_w1[l].rearrange("(k p) f -> p k f", p=P) for l in range(2)]
    w2_v = [mlp_w2[l].rearrange("(k p) d -> p k d", p=P) for l in range(2)]
    wpool_v = od_w_pool[0].rearrange("g (k p) d -> p (g k) d", p=P)
    x_in = [x_sample[0, 0:512].rearrange("(n p) d -> p n d", p=P),
            x_sample[0, 512:1024].rearrange("(n p) d -> p n d", p=P),
            x_prompt[0].rearrange("(n p) d -> p n d", p=P)]
    y_out = [y_sample[0, n * P:(n + 1) * P, :] for n in range(NS)] + [y_prompt[0, n * P:(n + 1) * P, :] for n in range(2)]

    def sem(name, n=None):
        return nc.alloc_semaphore(name) if n is None else [nc.alloc_semaphore(f"{name}{i}") for i in range(n)]

    const_in, x_loaded, ada0_in = sem("const_in"), sem("x_loaded", NTB), sem("ada0_in", 8)
    fill_ok, vec_mm, vec_ev, silu_ok = sem("fill_ok"), sem("vec_mm"), sem("vec_ev"), sem("silu_ok")
    dec_exp, dec_neg, dec_tab = sem("dec_exp"), sem("dec_neg"), sem("dec_tab")
    xt_mm, xt_ev, x_spilled, ada0_mm, mod_ok, gain_ok = (sem("xt_mm"), sem("xt_ev"), sem("x_spilled"), sem("ada0_mm"),
                                                         sem("mod_ok"), sem("gain_ok"))
    w_raw, w_hi, w_lo, a_raw, a_mm = sem("w_raw"), sem("w_hi"), sem("w_lo"), sem("a_raw"), sem("a_mm")
    sq_ok, sum_add, sum_mm, rms_ok, rstd_ok = sem("sq_ok"), sem("sum_add"), sem("sum_mm"), sem("rms_ok"), sem("rstd_ok")
    xn_ok, hs_ok, h_hi, h_lo = sem("xn_ok"), sem("hs_ok"), sem("h_hi"), sem("h_lo")
    in_mm, in_ev, ws_in, ws_mm, ws_ev = sem("in_mm"), sem("in_ev"), sem("ws_in"), sem("ws_mm"), sem("ws_ev")
    v_bn, v_stat, v_sd, v_rstd, v_norm = sem("v_bn"), sem("v_stat"), sem("v_sd"), sem("v_rstd"), sem("v_norm")
    sp_mm, t_ok, a_ok, a_hi, a_lo, a_spilled = (sem("sp_mm"), sem("t_ok"), sem("a_ok"), sem("a_hi"), sem("a_lo"),
                                                sem("a_spilled", 2))
    rope_in, swap_in, rot_s, rot_c, rot_ok, gate_out = (sem("rope_in"), sem("swap_in", 2), sem("rot_s"), sem("rot_c"),
                                                        sem("rot_ok"), sem("gate_out"))
    pos_in, tab_exp, tab_ok, state_in, zero_ok = sem("pos_in"), sem("tab_exp"), sem("tab_ok"), sem("state_in"), sem("zero_ok")
    kt_mm, kx_ok, kv_mm, s_ok, new_out = sem("kt_mm"), sem("kx_ok"), sem("kv_mm"), sem("s_ok"), sem("new_out")
    sc_mm, pt_ok, qd_ok, y_mm, y_bn, y_stat = sem("sc_mm"), sem("pt_ok"), sem("qd_ok"), sem("y_mm"), sem("y_bn"), sem("y_stat")
    y_sd, y_rstd, y_nmr, yn_ok, gate_in = sem("y_sd"), sem("y_rstd"), sem("y_nmr"), sem("yn_ok"), sem("gate_in", 2)
    gm_f, gm_b, b_ok, bt_mm, b_hi, b_lo = sem("gm_f"), sem("gm_b"), sem("b_ok"), sem("bt_mm"), sem("b_hi"), sem("b_lo")
    x_back, a_back, out_mm, out_ev = sem("x_back"), sem("a_back"), sem("out_mm"), sem("out_ev")
    pz_ok, pxn, ph, pw, pe_ok, pp = sem("pz_ok"), sem("pxn"), sem("ph"), sem("pw"), sem("pe_ok"), sem("pp")
    p_hi, p_lo, pool_mm, pool_ev = sem("p_hi"), sem("p_lo"), sem("pool_mm"), sem("pool_ev")
    m1_mm, relu_ok, sqr_ok, mid_hi, mid_lo = (sem("m1_mm", 2), sem("relu_ok", 2), sem("sqr_ok", 2), sem("mid_hi", 2),
                                              sem("mid_lo", 2))
    m2_mm, m2_ev = sem("m2_mm", 2), sem("m2_ev", 2)
    yn1_ok, yt_ok, yt_mm, yt_eva, yt_evv, y_done = (sem("yn1_ok"), sem("yt_ok"), sem("yt_mm"), sem("yt_eva"),
                                                    sem("yt_evv"), sem("y_done"))

    def cols(tb):
        t0, w, _ = TB[tb]
        return slice(t0, t0 + w)

    def pair_pass(out, w_hi_ap, w_lo_ap, m_hi_ap, m_lo_ap, first, last, weights_moving=False):
        if weights_moving:
            terms = ((m_hi_ap, w_hi_ap), (m_hi_ap, w_lo_ap), (m_lo_ap, w_hi_ap))
        else:
            terms = ((w_hi_ap, m_hi_ap), (w_hi_ap, m_lo_ap), (w_lo_ap, m_hi_ap))
        for n, (a, b) in enumerate(terms):
            mm = nc.tensor.matmul(out, a, b, start=first and n == 0, stop=last and n == 2)
        return mm

    X_READY = [(xt_ev, 0), (out_ev, 0), (m2_ev[0], GRP * (NCH - 1)), (pool_ev, 0), (m2_ev[1], GRP * (NCH - 1))]
    TURN = {0: 0, 1: 1, 3: 2}

    def total_bank(q, tb):
        return (bank[6], bank[5], bank[4])[tb] if q in TURN else (bank[6], bank[0], bank[1])[tb]

    def shift(q, d, cond):
        return mod[:, q // 2, 3 * DT * (q % 2) + d, cond:cond + 1]

    def pool_dst(d):
        return 1 + (d // 2) % 2

    def slot_free(U):
        if U < 2:
            return (ada0_mm, 2 * DT)
        if U <= U_OUT + 1:
            return (in_mm, IN_CUM[U - 1])
        if U <= U_MLP[0] + 1:
            return (out_mm, NTB * HT * (U - 2 - U_OUT + 1))
        if U == U_POOL:
            return (m1_mm[0], NTB * HT * NCH)
        if U == U_POOL + 1:
            return (m2_mm[0], GRP * NCH)
        return (pool_mm, GRP)

    block = ctx.enter_context(nc.Block())

    @block.sync
    def _(sp):
        def raw(U, view, split=DT):
            after(sp, w_lo, U)
            sp.dma_start(stage[:, :].rearrange("p (k n) -> p k n", k=split), view).then_inc(w_raw, 16)

        def raw_static(U):
            if U < U_OUT:
                raw(U, win_v[:, :, IN_UNITS[U][2]:IN_UNITS[U][2] + UC])
            elif U < U_MLP[0]:
                raw(U, wout_v[:, :, (U - U_OUT) * UC:(U - U_OUT + 1) * UC])
            elif U == U_POOL:
                raw(U, wpool_v)
            else:
                l = 1 if U > U_POOL else 0
                raw_mlp(l, (U - U_MLP[l]) // 2, (U - U_MLP[l]) % 2)

        def raw_mlp(l, ch, second):
            U = U_MLP[l] + 2 * ch + second
            if second:
                raw(U, w2_v[l][:, bass.ds(ch * HT, HT), :], HT)
            else:
                raw(U, w1_v[l][:, :, bass.ds(ch * UC, UC)])

        def ada_tile(n, l, col):
            after(sp, a_mm, n)
            sp.dma_start(ada_st[:, :, :], ada_v[l][:, :, bass.ds(col, P)]).then_inc(a_raw, 16)

        sp.dma_start(csm[:, :], small_const).then_inc(const_in, 16)
        vecs = [(0, c_ctx.rearrange("(k p) -> k p", p=P)), (8, c[0].rearrange("(k p) -> k p", p=P)),
                (16, norm_mix.rearrange("l (k p) -> (l k) p", p=P)), (32, norm_mlp.rearrange("l (k p) -> (l k) p", p=P)),
                (48, final_norm.rearrange("(k p) -> k p", p=P)), (56, od_pool_scale[0].rearrange("(k p) -> k p", p=P)),
                (64, ev_vnorm[0])]
        for r, v in vecs:
            sp.dma_start(rows[r:r + v.shape[0], :], v).then_inc(const_in, 16)
        sp.dma_start(ada_rows[0:2 * NMOD, :], ada_b.rearrange("l (k p) -> (l k) p", p=P)).then_inc(const_in, 16)
        sp.dma_start(dec[:, :], ev_decay.rearrange("o a h -> o (a h)").to_broadcast([P, 8])).then_inc(const_in, 16)
        for tb, adas in ((0, (0, 1, 2, 3)), (1, (4, 5, 6, 7)), (2, ())):
            n0, n1 = TB[tb][0] // P, (TB[tb][0] + TB[tb][1]) // P
            sp.dma_start(xtok[:, n0:n1, :], x_in[tb]).then_inc(x_loaded[tb], 16)
            for i in adas:
                sp.dma_start(ada0[i][:, :, :], ada_v[0][:, :, i * UC:(i + 1) * UC]).then_inc(ada0_in[i], 16)
        raw_static(0)
        raw_static(1)
        sp.wait_ge(xt_ev, GRP)
        sp.dma_start(x_dram, X[:, :, :]).then_inc(x_spilled, 16)
        n = 0
        for v in range(N_IN):
            tiles = min(3, ADA_IN - n)
            weights_after = tiles if v == 0 else min(tiles, 1)
            for j in range(tiles + 1):
                if j == weights_after and v + 2 <= U_OUT:
                    raw_static(v + 2)
                if j < tiles:
                    ada_tile(n, 0, (2 * DT + n) * P)
                    n += 1
            if v == 0:
                sp.wait_ge(h_lo, GRP)
                sp.dma_start(ws_raw[:, :, :], ev_w_s[0].rearrange("g i j -> i g j")).then_inc(ws_in, 16)
                sp.dma_start(bias_b[:, :, :].rearrange("p g i -> p (g i)"),
                             ev_b_s.rearrange("o g i -> o (g i)").to_broadcast([P, 4 * P])).then_inc(ws_in, 16)
            if IN_UNITS[v][0] == "u":
                for tb in range(NTB):
                    for f in range(HT):
                        i = (IN_UNITS[v][1] * NTB + tb) * HT + f
                        g, w = HT * IN_UNITS[v][1] + f, TB[tb][1]
                        sp.wait_ge(a_hi, i + 1)
                        sp.dma_start(a_dram[0][:, g, cols(tb)], gaH[i % 2][:, 0:w].bitcast(F32)).then_inc(a_spilled[i % 2], 16)
                        sp.wait_ge(a_lo, i + 1)
                        sp.dma_start(a_dram[1][:, g, cols(tb)], gaL[i % 2][:, 0:w].bitcast(F32)).then_inc(a_spilled[i % 2], 16)
                if IN_UNITS[v][1] == 1:
                    sp.wait_ge(sp_mm, 2 * NTB * HT)
                    sp.dma_start(rope[:, :, :], rope_const).then_inc(rope_in, 16)
            if v == 8:
                sp.wait_ge(rot_ok, 2 * HEADS)
                sp.dma_start(tab[:, :, :, :].rearrange("p a h i -> p (a h i)"), pos_const).then_inc(pos_in, 16)
        sp.wait_ge(in_mm, IN_CUM[N_IN])
        sp.dma_start(S[0][:, 0, :, :], state_ret[0, 0, 0].rearrange("h d e -> d h e")).then_inc(state_in, 16)
        sp.dma_start(S[1][:, NS - 1, :, :], state_ret[0, 0, 1].rearrange("h d e -> d h e")).then_inc(state_in, 16)
        sp.wait_ge(gate_out, 16 * 4)
        sp.wait_ge(w_lo, U_OUT + 1)
        for k in range(NT):
            after(sp, gm_f, k - 1)
            after(sp, gm_b, k - 1)
            for d in range(2):
                sp.dma_start(gt[k % 2][:, d, :, :],
                             g_dram[2 * d:2 * d + 2, :, k, :].rearrange("h p n -> p h n")).then_inc(gate_in[k % 2], 16)
            if k == 1:
                sp.wait_ge(s_ok, 2 * len(RSTEPS))
                for d in range(2):
                    sp.dma_start(new_state[0, 0, d].rearrange("h d e -> d h e"), new_st[:, d, :, :]).then_inc(new_out, 16)
        sp.wait_ge(gm_f, NT)
        sp.wait_ge(gm_b, NT)
        raw_static(U_OUT + 1)
        sp.wait_ge(bt_mm, NT)
        sp.wait_ge(a_spilled[0], 16 * 2 * NTB * HT)
        sp.wait_ge(a_spilled[1], 16 * 2 * NTB * HT)
        sp.dma_start(hH[:, 0:HEADS, :].bitcast(F32), a_dram[0]).then_inc(a_back, 16)
        sp.dma_start(hL[:, 0:HEADS, :].bitcast(F32), a_dram[1]).then_inc(a_back, 16)
        sp.wait_ge(x_spilled, 16)
        sp.dma_start(X[:, :, :], x_dram).then_inc(x_back, 16)
        for U in range(U_OUT + 2, U_MLP[0] + 2):
            raw_static(U)

        def mlp0_loads(ch, next0, next1):
            n0 = ADA_IN + ADA_PER_CHUNK * ch
            col = ADA_PER_CHUNK * P * ch
            ada_tile(n0, 1, col)
            next0()
            ada_tile(n0 + 1, 1, col + P)
            next1()
            ada_tile(n0 + 2, 1, col + 2 * P)

        with sp.Fori(0, NCH - 1) as ch:
            mlp0_loads(ch, lambda: raw_mlp(0, ch + 1, 0), lambda: raw_mlp(0, ch + 1, 1))
        mlp0_loads(NCH - 1, lambda: raw_static(U_POOL), lambda: raw_static(U_MLP[1]))
        raw_static(U_MLP[1] + 1)
        with sp.Fori(1, NCH) as ch:
            raw_mlp(1, ch, 0)
            raw_mlp(1, ch, 1)
        for n in range(NT):
            sp.wait_ge(yt_eva, n + 1)
            sp.wait_ge(yt_evv, n + 1)
            sp.dma_start(y_out[n], ytok[:, n, :]).then_inc(y_done, 16)
        sp.wait_ge(new_out, 32)
        sp.wait_ge(y_done, 16 * NT)

    @block.scalar
    def _(act):
        def split_hi(U, free, slot):
            act.wait_ge(w_raw, 16 * (U + 1))
            act.wait_ge(*free)
            nc.scalar.activation(ringH[slot][:, :], stage[:, :], ACT.Copy).then_inc(w_hi, 1)

        def split_static(U):
            split_hi(U, slot_free(U), U % 2)

        def square(q, i):
            t, d = NORM_ORDER[q][i]
            add, w = ADDS[q][(t, d)], TB[t][1]
            ready, base_n = X_READY[q]
            act.wait_ge(ready, base_n + i + 1)
            if add is None:
                dst = acc2[q % 2][:, cols(t)]
            else:
                after(act, sum_add, ADDS_PER_NORM * q + add - 1)
                dst = sq_b[add % 2][:, 0:w]
            nc.scalar.activation(dst, X[:, d, cols(t)], ACT.Square).then_inc(sq_ok, 1)

        def rms(q, tb):
            act.wait_ge(sum_mm, NTB * q + tb + 1)
            nc.scalar.activation(acc2[q % 2][:, cols(tb)], total_bank(q, tb)[:, 0:TB[tb][1]], ACT.Sqrt, bias=eps_t[:, :],
                                 scale=1.0 / D).then_inc(rms_ok, 1)

        def apply_hi(q, tb):
            rms(q, tb)
            for d in range(DT):
                i = GRP * TURN[q] + DT * tb + d
                act.wait_ge(hs_ok, i + 1)
                nc.scalar.activation(hH[:, d, cols(tb)], hs_b[i % 2][:, 0:TB[tb][1]], ACT.Copy).then_inc(h_hi, 1)

        act.wait_ge(const_in, 16 * 10)
        nc.scalar.activation(dec[:, :], dec[:, :], ACT.Exp).then_inc(dec_exp, 1)
        act.wait_ge(dec_neg, 1)
        nc.scalar.activation(kd[:, 0:4], ned[:, 0:4], ACT.Exp, scale=csm[:, P:P + 1]).then_inc(dec_tab, 1)
        nc.scalar.activation(kd[:, 4:8], ned[:, 4:8], ACT.Exp, scale=csm[:, P + 1:P + 2]).then_inc(dec_tab, 1)
        nc.scalar.activation(cd[:, :], ned[:, :], ACT.Exp, scale=float(P)).then_inc(dec_tab, 1)
        act.wait_ge(vec_ev, 1)
        nc.scalar.activation(sc2[:, :, :].rearrange("p k c -> p c k"), vec[:, 0:16].rearrange("p (c k) -> p c k", c=2),
                             ACT.Silu).then_inc(silu_ok, 1)
        for i in range(GRP):
            square(0, i)
        act.wait_ge(w_raw, 16)
        nc.scalar.activation(ringH[0][:, :], stage[:, :], ACT.Copy).then_inc(w_hi, 1)
        act.wait_ge(fill_ok, 2)

        G, gates = 0, 0
        for ui, (kind, half, _, tok) in enumerate(IN_UNITS):
            for g in range(IN_GROUPS[ui]):
                if ui == 0 and g in (0, 4, 8):
                    apply_hi(0, g // 4)
                if ui == 11 and g == 1:
                    act.wait_ge(pos_in, 16)
                    for a in range(4):
                        for h in range(HEADS):
                            e = nc.scalar.activation(tab[:, a, h, :], tab[:, a, h, :], ACT.Exp,
                                                     scale=ned[:, 4 * (a % 2) + h:4 * (a % 2) + h + 1])
                    e.then_inc(tab_exp, 1)
                act.wait_ge(in_mm, G + 1)
                if tok:
                    src = bank[G % 4][:, 0:UC]
                    lo, hi = half * UC, (half + 1) * UC
                    if kind == "v":
                        ev = nc.scalar.activation(vtok[:, g, lo:hi], src, ACT.Gelu_apprx_tanh)
                    elif kind == "val":
                        if half == 0 and g == 0:
                            for s in a_spilled:
                                act.wait_ge(s, 16 * 2 * NTB * HT)
                        ev = nc.scalar.activation(val[:, g, lo:hi], src, ACT.Copy)
                    else:
                        if g == 0:
                            act.wait_ge(rot_ok, 2 * HEADS)
                            after(act, gate_out, 16 * gates)
                        ev = nc.scalar.activation(gate_st[:, g, :], src, ACT.Silu)
                else:
                    tb, f = g // HT, g % HT
                    w = TB[tb][1]
                    src = bank[G % 4][:, 0:w]
                    if kind == "u":
                        i = (half * NTB + tb) * HT + f
                        if i == 0:
                            act.wait_ge(ws_ev, 1)
                        after(act, a_ok, i - 1)
                        ev = nc.scalar.activation(ug[i % 2][:, 0:w], src, ACT.Gelu_apprx_tanh)
                    else:
                        if kind == "q" and half == 0 and g == 0:
                            act.wait_ge(x_spilled, 16)
                        hd = (HEADS if kind == "k" else 0) + HT * half + f
                        ev = nc.scalar.activation(qk[:, hd, cols(tb)], src, ACT.Copy,
                                                  scale=float(P) ** -0.5 if kind == "k" else 1.0)
                ev.then_inc(in_ev, 1)
                G += 1
                if kind in "qk" and tb == 1:
                    if hd == 0:
                        act.wait_ge(sp_mm, 2 * NTB * HT)
                    after(act, rot_ok, hd - 1)
                    act.wait_ge(in_ev, G)
                    for a, b in ((0, P // 2), (P // 2, 0)):
                        act.dma_start(swap[hd % 2][a:a + P // 2, :], qk[b:b + P // 2, hd, 0:SAMPLE]).then_inc(swap_in[hd % 2], 16)
                if g == 0:
                    split_static(ui + 1)
            if kind == "v" and half == 1:
                act.wait_ge(v_stat, NT)
                nc.scalar.activation(vmv[:, :, 1], vmv[:, :, 1], ACT.Sqrt, bias=eps_t[:, :]).then_inc(v_sd, 1)
            if kind in ("gf", "gb"):
                act.wait_ge(in_ev, G)
                act.dma_start(g_dram[gates], gate_st[:, :, :]).then_inc(gate_out, 16)
                gates += 1

        for k in range(NT + 3):
            n = k - 1
            if 0 <= n < NT:
                act.wait_ge(y_stat, n + 1)
                nc.scalar.activation(rmv[n % 2][:, :, 1], rmv[n % 2][:, :, 1], ACT.Sqrt, bias=eps_t[:, :]).then_inc(y_sd, 1)
            m = k - 3
            if 0 <= m < NT:
                act.wait_ge(bt_mm, m + 1)
                nc.scalar.activation(hH[:, HEADS:DT, m * P:(m + 1) * P],
                                     bank[6 + m % 2][:, :].rearrange("p (h i) -> p h i", h=HEADS), ACT.Copy).then_inc(b_hi, 1)
            if 0 <= n < NT:
                act.wait_ge(y_nmr, n + 1)
                after(act, bt_mm, n - 1)
                if n == 0:
                    act.wait_ge(new_out, 32)
                for d in range(2):
                    for h in range(HEADS):
                        j = HEADS * d + h
                        ev = nc.scalar.activation(yn[n % 2][:, d, h, :], bank[2 + 2 * (n % 2) + d][:, h * P:(h + 1) * P],
                                                  ACT.Identity, scale=rmv[n % 2][:, j, 1:2], bias=rnm[n % 2][:, j:j + 1])
                    ev.then_inc(yn_ok, 1)

        act.wait_ge(bt_mm, NT)
        split_static(U_OUT + 1)
        for u in range(N_OUT):
            for i in range(NTB * HT * u, NTB * HT * (u + 1)):
                square(1, i)
            if u < N_OUT - 1:
                split_static(U_OUT + 2 + u)

        def mlp(l, ch, first=False, last=False):
            q = 2 * l + 1
            U = U_MLP[l] + 2 * ch
            n0 = NTB * HT * ch

            def hidden_hi(g):
                act.wait_ge(sqr_ok[l], n0 + g + 1)
                if g == 0:
                    after(act, m2_mm[l], GRP * ch)
                act_ = nc.scalar.activation(midH[:, g % HT, cols(g // HT)], r_b[g % 3][:, 0:TB[g // HT][1]], ACT.Copy)
                act_.then_inc(mid_hi[l], 1)

            if first:
                apply_hi(q, 0)
                apply_hi(q, 1)
            for g in range(NTB * HT):
                if first and g == 2:
                    apply_hi(q, 2)
                act.wait_ge(m1_mm[l], n0 + g + 1)
                after(act, mid_lo[l], n0 + g - 2)
                nc.scalar.activation(r_b[g % 3][:, 0:TB[g // HT][1]], bank[g % 2][:, 0:TB[g // HT][1]],
                                     ACT.Relu).then_inc(relu_ok[l], 1)
                if g == 0:
                    split_hi(U + 1, slot_free(U_MLP[l] + 1) if first else (m2_mm[l], GRP * ch), (U_MLP[l] + 1) % 2)
                if g > 0:
                    hidden_hi(g - 1)
            hidden_hi(NTB * HT - 1)
            if not (l == 1 and last):
                split_hi(U + 2, (m1_mm[l], NTB * HT * (ch + 1)), U_MLP[l] % 2)
            if last:
                for i in range(GRP):
                    square(2 * l + 2, i)
                    if i == 2 * DT - 1:
                        rms(2 * l + 2, 0)
                rms(2 * l + 2, 1)
                rms(2 * l + 2, 2)

        mlp(0, 0, first=True)
        with act.Fori(1, NCH - 1) as ch:
            mlp(0, ch)
        mlp(0, NCH - 1, last=True)

        segs = ((PADW, 0, SAMPLE, 1), (SAMPLE + 3 * PADW, SAMPLE, PROMPT, 0))
        split_static(U_MLP[1])

        def pool_hs(d):
            act.wait_ge(pxn, d + 1)
            for p0, t0, w, cond in segs:
                a = prow[d % 2][0][:, p0:p0 + w]
                e = nc.scalar.activation(a, a, ACT.Identity, scale=gain[2][:, d, cond:cond + 1], bias=shift(2, d, cond))
            e.then_inc(ph, 1)

        def pool_hi(d):
            act.wait_ge(pp, d + 1)
            for p0, t0, w, cond in segs:
                e = nc.scalar.activation(hH[:, d, t0:t0 + w], prow[d % 2][pool_dst(d)][:, p0:p0 + w], ACT.Copy)
            e.then_inc(p_hi, 1)

        act.wait_ge(gain_ok, 4)
        pool_hs(0)
        for d in range(DT):
            if d + 1 < DT:
                pool_hs(d + 1)
            pool_hi(d)
            if d >= 3 and d % 2 == 1:
                for i in range(6 * (d // 2 - 1), 6 * (d // 2)):
                    square(3, i)
        for i in range(6 * (DT // 2 - 1), GRP):
            square(3, i)

        mlp(1, 0, first=True)
        with act.Fori(1, NCH - 1) as ch:
            mlp(1, ch)
        mlp(1, NCH - 1, last=True)
        for n in range(NT):
            act.wait_ge(yt_mm, 2 * n + 1)
            nc.scalar.activation(ytok[:, n, 0:512], bank[(2 * n) % 4][:, :], ACT.Copy).then_inc(yt_eva, 1)

    @block.gpsimd
    def _(pool):
        def split_lo(U, slot=None):
            slot = U % 2 if slot is None else slot
            pool.wait_ge(w_hi, U + 1)
            nc.gpsimd.tensor_tensor(ringL[slot][:, :], stage[:, :], ringH[slot][:, :].bitcast(F32),
                                    ALU.subtract).then_inc(w_lo, 1)

        def add_square(q, i):
            t, d = NORM_ORDER[q][i]
            add = ADDS[q][(t, d)]
            if add is None:
                return
            pool.wait_ge(sq_ok, GRP * q + i + 1)
            after(pool, sum_add, ADDS_PER_NORM * q + add)
            nc.gpsimd.tensor_tensor(acc2[q % 2][:, cols(t)], acc2[q % 2][:, cols(t)], sq_b[add % 2][:, 0:TB[t][1]], ALU.add).then_inc(sum_add, 1)

        def apply_xn(q, tb):
            pool.wait_ge(rstd_ok, NTB * q + tb + 1)
            for d in range(DT):
                i = GRP * TURN[q] + DT * tb + d
                after(pool, hs_ok, i - 1)
                nc.gpsimd.tensor_tensor(xn_b[i % 2][:, 0:TB[tb][1]], X[:, d, cols(tb)], acc2[q % 2][:, cols(tb)],
                                        ALU.mult).then_inc(xn_ok, 1)

        nc.gpsimd.memset(ones[:, :], 1.0).then_inc(fill_ok, 1)
        nc.gpsimd.memset(eps_t[:, :], EPS).then_inc(fill_ok, 1)
        for i in range(GRP):
            add_square(0, i)
        split_lo(0)
        for tb in range(NTB):
            apply_xn(0, tb)
        for ui, (kind, half, _, tok) in enumerate(IN_UNITS):
            split_lo(ui + 1)
            if kind == "u":
                for g in range(NTB * HT):
                    i, w = NTB * HT * half + g, TB[g // HT][1]
                    pool.wait_ge(a_ok, i + 1)
                    after(pool, a_spilled[i % 2], 32 * (i // 2))
                    nc.gpsimd.tensor_copy(gaH[i % 2][:, 0:w], ga[i % 2][:, 0:w]).then_inc(a_hi, 1)
                    pool.wait_ge(a_hi, i + 1)
                    nc.gpsimd.tensor_tensor(gaL[i % 2][:, 0:w], ga[i % 2][:, 0:w], gaH[i % 2][:, 0:w].bitcast(F32),
                                            ALU.subtract).then_inc(a_lo, 1)
            if kind in "qk":
                for hd in ((HEADS if kind == "k" else 0) + HT * half + f for f in range(HT)):
                    pool.wait_ge(rope_in, 16)
                    pool.wait_ge(swap_in[hd % 2], 32 * (hd // 2 + 1))
                    nc.gpsimd.tensor_tensor(qk[:, hd, 0:SAMPLE], qk[:, hd, 0:SAMPLE], rope[:, 0, :], ALU.mult).then_inc(rot_c, 1)
        pool.wait_ge(tab_exp, 1)
        for a, sign in ((0, 1), (1, -1)):
            nc.gpsimd.affine_select(out=tab[:, a, :, :], in_=tab[:, a, :, :], compare_op=ALU.is_ge, fill=0.0, base=0,
                                    pattern=[[0, HEADS], [sign, P]], channel_multiplier=-sign).then_inc(tab_ok, 1)
        pool.wait_ge(in_mm, IN_CUM[N_IN])
        nc.gpsimd.memset(S[0][:, NS, :, :], 0.0).then_inc(zero_ok, 1)
        nc.gpsimd.memset(S[1][:, NS + 1, :, :], 0.0).then_inc(zero_ok, 1)
        pool.wait_ge(tab_ok, 2)
        for k in range(NT + 2):
            if k < NT:
                after(pool, y_mm, 2 * (k - 1))
                for d in range(2):
                    nc.gpsimd.tensor_tensor(qd[k % 2][:, d, :, :], qk[:, 0:HEADS, k * P:(k + 1) * P], tab[:, 2 + d, :, :],
                                            ALU.mult).then_inc(qd_ok, 1)
            n = k - 2
            if n >= 0:
                pool.wait_ge(yn_ok, 2 * n + 2)
                pool.wait_ge(gate_in[n % 2], 32 * (n // 2 + 1))
                y1 = yn[n % 2][:, 1, :, :].rearrange("p h e -> p (h e)")
                nc.gpsimd.tensor_tensor(y1, y1, gt[n % 2][:, 1, :, :].rearrange("p a n -> p (a n)"), ALU.mult).then_inc(gm_b, 1)
        split_lo(U_OUT + 1)
        for u in range(N_OUT):
            for i in range(NTB * HT * u, NTB * HT * (u + 1)):
                add_square(1, i)
            if u < N_OUT - 1:
                split_lo(U_OUT + 2 + u)

        def mlp(l, ch, first=False, last=False):
            if first:
                for tb in range(NTB):
                    apply_xn(2 * l + 1, tb)
            split_lo(U_MLP[l] + 2 * ch + 1, (U_MLP[l] + 1) % 2)
            if not (l == 1 and last):
                split_lo(U_MLP[l] + 2 * ch + 2, U_MLP[l] % 2)
            if last:
                for i in range(GRP):
                    add_square(2 * l + 2, i)

        mlp(0, 0, first=True)
        with pool.Fori(1, NCH - 1) as ch:
            mlp(0, ch)
        mlp(0, NCH - 1, last=True)

        segs = ((PADW, 0, SAMPLE), (SAMPLE + 3 * PADW, SAMPLE, PROMPT))
        pool.wait_ge(m2_mm[0], GRP * NCH)
        for i in range(2):
            for p0, w in ((0, PADW), (PADW + SAMPLE, 2 * PADW), (PW - PADW, PADW)):
                z = nc.gpsimd.memset(prow[i][0][:, p0:p0 + w], 0.0)
        z.then_inc(pz_ok, 1)
        split_lo(U_MLP[1])
        pool.wait_ge(rstd_ok, NTB * 3)

        def pool_xn(d):
            after(pool, p_lo, d - 1)
            for p0, t0, w in segs:
                e = nc.gpsimd.tensor_tensor(prow[d % 2][0][:, p0:p0 + w], X[:, d, t0:t0 + w], acc2[0][:, t0:t0 + w], ALU.mult)
            e.then_inc(pxn, 1)

        def pool_lo(d):
            pool.wait_ge(p_hi, d + 1)
            for p0, t0, w in segs:
                e = nc.gpsimd.tensor_tensor(hL[:, d, t0:t0 + w], prow[d % 2][pool_dst(d)][:, p0:p0 + w],
                                            hH[:, d, t0:t0 + w].bitcast(F32), ALU.subtract)
            e.then_inc(p_lo, 1)

        pool_xn(0)
        pool_xn(1)
        for d in range(DT):
            pool_lo(d)
            if d + 2 < DT:
                pool_xn(d + 2)
            if d >= 3 and d % 2 == 1:
                for i in range(6 * (d // 2 - 1), 6 * (d // 2)):
                    add_square(3, i)
        for i in range(6 * (DT // 2 - 1), GRP):
            add_square(3, i)

        mlp(1, 0, first=True)
        with pool.Fori(1, NCH - 1) as ch:
            mlp(1, ch)
        mlp(1, NCH - 1, last=True)

    @block.vector
    def _(dve):
        V = nc.vector

        def rstd(q, tb):
            dve.wait_ge(rms_ok, NTB * q + tb + 1)
            V.reciprocal(acc2[q % 2][:, cols(tb)], acc2[q % 2][:, cols(tb)]).then_inc(rstd_ok, 1)

        def gains(q, dst=None):
            l, m = q // 2, q % 2
            v0 = (32 if m else 16) + DT * l
            V.scalar_tensor_tensor(out=gain[q][:, :, :], in0=mod[:, l, 3 * DT * m + DT:3 * DT * m + 2 * DT, :], scalar=1.0,
                                   in1=vec[:, v0:v0 + DT].unsqueeze(2).to_broadcast([P, DT, 2]),
                                   op0=ALU.add, op1=ALU.mult).then_inc(gain_ok, 1)

        def mods(l, j0, j1, col, nth):
            V.tensor_tensor(mod[:, l, j0:j1, :], ADA_BANK[:, col:col + 2 * (j1 - j0)].rearrange("p (j c) -> p j c", c=2),
                            adab[:, NMOD * l + j0:NMOD * l + j1].unsqueeze(2).to_broadcast([P, j1 - j0, 2]),
                            ALU.add).then_inc(mod_ok, 1)
            dve.wait_ge(mod_ok, nth)

        def apply(q, tb):
            rstd(q, tb)
            w, cond = TB[tb][1:]

            def lower(d):
                i = GRP * TURN[q] + DT * tb + d
                dve.wait_ge(h_hi, i + 1)
                V.tensor_tensor(hL[:, d, cols(tb)], hs_b[i % 2][:, 0:w], hH[:, d, cols(tb)].bitcast(F32),
                                ALU.subtract).then_inc(h_lo, 1)

            for d in range(DT):
                i = GRP * TURN[q] + DT * tb + d
                dve.wait_ge(xn_ok, i + 1)
                after(dve, h_lo, i - 1)
                V.tensor_scalar(hs_b[i % 2][:, 0:w], xn_b[i % 2][:, 0:w], gain[q][:, d, cond:cond + 1], shift(q, d, cond),
                                ALU.mult, ALU.add).then_inc(hs_ok, 1)
                if d > 0:
                    lower(d - 1)
            lower(DT - 1)

        def update(mm, n, ev, src, gate_ap, t, d, own):
            dve.wait_ge(mm, n)
            if own is not None:
                after(dve, *own)
            V.scalar_tensor_tensor(out=X[:, d, cols(t)], in0=src[:, 0:TB[t][1]], scalar=gate_ap, in1=X[:, d, cols(t)],
                                   op0=ALU.mult, op1=ALU.add).then_inc(ev, 1)

        dve.wait_ge(dec_exp, 1)
        V.tensor_scalar(ned[:, :], dec[:, :], -1.0, None, ALU.mult).then_inc(dec_neg, 1)
        dve.wait_ge(vec_mm, 1)
        V.tensor_copy(vec[:, :], bank[5][:, 0:68]).then_inc(vec_ev, 1)
        dve.wait_ge(vec_mm, 2)
        V.tensor_copy(adab[:, :], bank[4][:, 0:2 * NMOD]).then_inc(vec_ev, 1)
        for i, (t, d) in enumerate(BY_BLOCK):
            dve.wait_ge(xt_mm, i + 1)
            V.tensor_copy(X[:, d, cols(t)], bank[i % 4][:, 0:TB[t][1]]).then_inc(xt_ev, 1)
        dve.wait_ge(ada0_mm, 2 * DT)
        dve.wait_ge(vec_ev, 2)
        mods(0, 0, 2 * DT, 0, 1)
        gains(0)
        dve.wait_ge(gain_ok, 1)
        for tb in range(NTB):
            apply(0, tb)
        dve.wait_ge(ws_mm, 1)
        V.tensor_copy(wsT[:, :, :].rearrange("p g i -> p (g i)"), WS_BANK[:, :]).then_inc(ws_ev, 1)
        for n in range(NT):
            dve.wait_ge(in_ev, IN_CUM[1] + n + 1)
            for g in range(4):
                e = V.bn_stats(vst[:, 4 * n + g, :], vtok[:, n, g * P:(g + 1) * P])
            e.then_inc(v_bn, 1)
            dve.wait_ge(v_bn, n + 1)
            for g in range(4):
                e = V.bn_aggr(vmv[:, 4 * n + g, :], vst[:, 4 * n + g, :])
            e.then_inc(v_stat, 1)
        dve.wait_ge(v_sd, 1)
        V.reciprocal(vmv[:, :, 1], vmv[:, :, 1]).then_inc(v_rstd, 1)
        dve.wait_ge(v_rstd, 1)
        for n in range(NT):
            for g in range(4):
                a, j = vtok[:, n, g * P:(g + 1) * P], 4 * n + g
                e = V.tensor_scalar(a, a, vmv[:, j, 0:1], vmv[:, j, 1:2], ALU.subtract, ALU.mult)
            e.then_inc(v_norm, 1)
        dve.wait_ge(ws_in, 32)
        for half in range(HT):
            for g6 in range(NTB * HT):
                i, tb = NTB * HT * half + g6, g6 // HT
                g, w = HT * half + g6 % HT, TB[tb][1]
                dve.wait_ge(sp_mm, i + 1)
                after(dve, a_lo, i - 1)
                chunks = dict(c=w // P)
                V.scalar_tensor_tensor(out=ga[i % 2][:, 0:w].rearrange("p (c i) -> p c i", **chunks),
                                       in0=bank[4 + i % 2][:, 0:w].rearrange("p (c i) -> p c i", **chunks),
                                       scalar=vec[:, 64 + g:65 + g],
                                       in1=bias_b[:, g, :].unsqueeze(1).to_broadcast([P, w // P, P]),
                                       op0=ALU.mult, op1=ALU.add).then_inc(t_ok, 1)
                dve.wait_ge(t_ok, i + 1)
                dve.wait_ge(in_ev, IN_CUM[2 + half] + g6 + 1)
                V.tensor_tensor(ga[i % 2][:, 0:w], ga[i % 2][:, 0:w], ug[i % 2][:, 0:w], ALU.mult).then_inc(a_ok, 1)
        dve.wait_ge(rope_in, 16)
        for hd in range(2 * HEADS):
            dve.wait_ge(swap_in[hd % 2], 32 * (hd // 2 + 1))
            V.tensor_tensor(swap[hd % 2][:, :], swap[hd % 2][:, :], rope[:, 1, :], ALU.mult).then_inc(rot_s, 1)
            dve.wait_ge(rot_s, hd + 1)
            dve.wait_ge(rot_c, hd + 1)
            V.tensor_tensor(qk[:, hd, 0:SAMPLE], qk[:, hd, 0:SAMPLE], swap[hd % 2][:, :], ALU.add).then_inc(rot_ok, 1)
        dve.wait_ge(a_mm, ADA_IN)
        mods(0, 2 * DT, NMOD, 4 * DT, 2)
        gains(1)

        dve.wait_ge(dec_tab, 3)
        dve.wait_ge(gate_out, 16 * 4)

        def key_decay(s):
            for d in range(2):
                dve.wait_ge(kt_mm, 2 * s + d + 1)
                after(dve, kv_mm, 2 * (s - 2) + d + 1)
                V.tensor_tensor(kx[s % 2][:, d, :, :], bank[2 * (s % 2) + d][:, :].rearrange("p (h e) -> p h e", h=HEADS),
                                kd[:, 4 * d:4 * d + 4].unsqueeze(2).to_broadcast([P, HEADS, P]), ALU.mult).then_inc(kx_ok, 1)

        def state_step(s):
            for d in range(2):
                n = RSTEPS[s][d]
                dve.wait_ge(kv_mm, 2 * s + d + 1)
                after(dve, s_ok, 2 * (s - 1) + d + 1)
                final = (n == NS + 1) if d == 0 else (n == NS)
                final = final and s == len(RSTEPS) - 1
                for h in range(HEADS):
                    dst = new_st[:, d, h, :] if final else S[d][:, n + 1 - 2 * d, h, :]
                    e = V.scalar_tensor_tensor(out=dst, in0=S[d][:, n, h, :], scalar=cd[:, 4 * d + h:4 * d + h + 1],
                                               in1=bank[4 + 2 * (s % 2) + d][:, h * P:(h + 1) * P],
                                               op0=ALU.mult, op1=ALU.add)
                e.then_inc(s_ok, 1)

        dve.wait_ge(state_in, 32)
        dve.wait_ge(zero_ok, 2)
        for s in range(len(RSTEPS) + 1):
            if s < len(RSTEPS):
                key_decay(s)
            if s > 0:
                state_step(s - 1)
        dve.wait_ge(tab_ok, 2)
        for k in range(NT + 3):
            n = k - 1
            if 0 <= n < NT:
                for d in range(2):
                    dve.wait_ge(y_mm, 2 * n + d + 1)
                    for h in range(HEADS):
                        e = V.bn_stats(rst[n % 2][:, HEADS * d + h, :], bank[2 + 2 * (n % 2) + d][:, h * P:(h + 1) * P])
                e.then_inc(y_bn, 1)
                dve.wait_ge(y_bn, n + 1)
                after(dve, yn_ok, 2 * (n - 1))
                for j in range(2 * HEADS):
                    e = V.bn_aggr(rmv[n % 2][:, j, :], rst[n % 2][:, j, :])
                e.then_inc(y_stat, 1)
            if k < NT:
                dve.wait_ge(sc_mm, k + 1)
                after(dve, y_mm, 2 * (k - 1))
                for d in range(2):
                    V.tensor_tensor(pt[k % 2][:, d, :, :], bank[k % 2][:, :].rearrange("p (h i) -> p h i", h=HEADS),
                                    tab[:, d, :, :], ALU.mult).then_inc(pt_ok, 1)
            if 0 <= n < NT:
                dve.wait_ge(y_sd, n + 1)
                V.reciprocal(rmv[n % 2][:, :, 1], rmv[n % 2][:, :, 1]).then_inc(y_rstd, 1)
                dve.wait_ge(y_rstd, n + 1)
                V.scalar_tensor_tensor(out=rnm[n % 2][:, :], in0=rmv[n % 2][:, :, 0], scalar=-1.0, in1=rmv[n % 2][:, :, 1],
                                       op0=ALU.mult, op1=ALU.mult).then_inc(y_nmr, 1)
            m = k - 2
            if 0 <= m < NT:
                dve.wait_ge(yn_ok, 2 * m + 2)
                dve.wait_ge(gate_in[m % 2], 32 * (m // 2 + 1))
                y0, y1 = (yn[m % 2][:, d, :, :].rearrange("p h e -> p (h e)") for d in range(2))
                V.tensor_tensor(y0, y0, gt[m % 2][:, 0, :, :].rearrange("p a n -> p (a n)"), ALU.mult).then_inc(gm_f, 1)
                dve.wait_ge(gm_f, m + 1)
                dve.wait_ge(gm_b, m + 1)
                V.tensor_tensor(y0, y0, y1, ALU.add).then_inc(b_ok, 1)
            m = k - 3
            if 0 <= m < NT:
                dve.wait_ge(b_hi, m + 1)
                V.tensor_tensor(hL[:, HEADS:DT, m * P:(m + 1) * P], bank[6 + m % 2][:, :].rearrange("p (h i) -> p h i", h=HEADS),
                                hH[:, HEADS:DT, m * P:(m + 1) * P].bitcast(F32), ALU.subtract).then_inc(b_lo, 1)

        dve.wait_ge(x_back, 16)
        dve.wait_ge(mod_ok, 2)
        for i, (t, d) in enumerate(BY_PAIR):
            update(out_mm, i + 1, out_ev, bank[i % 4], mod[:, 0, 2 * DT + d, TB[t][2]:TB[t][2] + 1], t, d, None)

        def mlp(l, ch, first=False, last=False):
            n0 = NTB * HT * ch

            def hidden_lo(g):
                dve.wait_ge(mid_hi[l], n0 + g + 1)
                w = TB[g // HT][1]
                V.tensor_tensor(midL[:, g % HT, cols(g // HT)], r_b[g % 3][:, 0:w],
                                midH[:, g % HT, cols(g // HT)].bitcast(F32), ALU.subtract).then_inc(mid_lo[l], 1)

            if first:
                dve.wait_ge(gain_ok, 2 if l == 0 else 5)
                apply(2 * l + 1, 0)
                apply(2 * l + 1, 1)
            for g in range(NTB * HT):
                if first and g == 2:
                    apply(2 * l + 1, 2)
                dve.wait_ge(relu_ok[l], n0 + g + 1)
                r = r_b[g % 3][:, 0:TB[g // HT][1]]
                V.tensor_tensor(r, r, r, ALU.mult).then_inc(sqr_ok[l], 1)
                if g > 0:
                    hidden_lo(g - 1)
            hidden_lo(NTB * HT - 1)
            for i, (t, d) in enumerate(BY_BLOCK):
                n = GRP * ch + i
                update(m2_mm[l], n + 1, m2_ev[l], bank[2 + i % 4], mod[:, l, 5 * DT + d, TB[t][2]:TB[t][2] + 1], t, d,
                       (m2_ev[l], n + 1 - GRP))
                if last and i == 2 * DT - 1:
                    rstd(2 * l + 2, 0)
            if last:
                rstd(2 * l + 2, 1)
                rstd(2 * l + 2, 2)

        mlp(0, 0, first=True)
        with dve.Fori(1, NCH - 1) as ch:
            mlp(0, ch)
        mlp(0, NCH - 1, last=True)

        dve.wait_ge(a_mm, ADA_IN + NMOD)
        mods(1, 0, NMOD, 0, 3)
        gains(2)
        V.tensor_tensor(gpool[:, :, :], mod[:, 1, 2 * DT:3 * DT, :], vec[:, 56:56 + DT].unsqueeze(2).to_broadcast([P, DT, 2]),
                        ALU.mult).then_inc(gain_ok, 1)
        gains(3)
        dve.wait_ge(gain_ok, 5)

        def pooled(d):
            g = d // 2
            row = prow[d % 2]
            dve.wait_ge(ph, d + 1)
            steps = [(1, 0, (1, PW), 1, 0), (2, 1, (2, PW - 1), 1, 1), (1, 2, (4, PW - 3), 2, 2), (2, 1, (8, PW - 7), 4, 4)]
            for dst, src, (a, b), back, ahead in steps[:g + 1]:
                V.tensor_tensor(row[dst][:, a:b], row[src][:, a - back:b - back], row[src][:, a + ahead:b + ahead],
                                ALU.add).then_inc(pw, 1)
                pw_n[0] += 1
                dve.wait_ge(pw, pw_n[0])
            res = row[pool_dst(d)]
            for p0, w in ((PADW, SAMPLE), (SAMPLE + 3 * PADW, PROMPT)):
                for side, a in ((0, p0), (1, p0 + w - PADW)):
                    e = V.tensor_tensor(res[:, a:a + PADW], res[:, a:a + PADW], edges[:, g, side, :], ALU.mult)
            e.then_inc(pe_ok, 1)
            dve.wait_ge(pe_ok, d + 1)
            V.scalar_tensor_tensor(out=res[:, PADW:PW - PADW], in0=res[:, PADW:PW - PADW], scalar=1.0 / WINDOWS[g],
                                   in1=row[0][:, PADW:PW - PADW], op0=ALU.mult, op1=ALU.subtract).then_inc(pp, 1)

        def pool_updates(g):
            for i in range(6 * g, 6 * (g + 1)):
                t, d = BY_PAIR[i]
                update(pool_mm, i + 1, pool_ev, bank[i % 4], gpool[:, d, TB[t][2]:TB[t][2] + 1], t, d, None)

        pw_n = [0]
        dve.wait_ge(pz_ok, 1)
        for d in range(DT):
            pooled(d)
            if d >= 3 and d % 2 == 1:
                pool_updates(d // 2 - 1)
        pool_updates(DT // 2 - 1)

        mlp(1, 0, first=True)
        with dve.Fori(1, NCH - 1) as ch:
            mlp(1, ch)
        mlp(1, NCH - 1, last=True)

        dve.wait_ge(rstd_ok, NTB * 5)
        for t, d in BY_BLOCK:
            V.scalar_tensor_tensor(out=yT[:, d, cols(t)], in0=X[:, d, cols(t)], scalar=vec[:, 48 + d:49 + d],
                                   in1=acc2[0][:, cols(t)], op0=ALU.mult, op1=ALU.mult).then_inc(yt_ok, 1)
        for n in range(NT):
            dve.wait_ge(yt_mm, 2 * n + 2)
            V.tensor_copy(ytok[:, n, 512:1024], bank[(2 * n + 1) % 4][:, :]).then_inc(yt_evv, 1)

    @block.tensor
    def _(pe):
        def ada_mult(wt, out_ap, count):
            for k in range(DT):
                mm = nc.tensor.matmul(out_ap, wt(k), sc2[:, k, :], start=(k == 0), stop=(k == DT - 1))
            mm.then_inc(count, 1)

        def ada_tile(n, col):
            pe.wait_ge(a_raw, 16 * (n + 1))
            ada_mult(lambda k: ada_st[:, k, :], ADA_BANK[:, col], a_mm)

        def total(q, tb):
            need = 1 + max(a for (t, d), a in ADDS[q].items() if t == tb and a is not None)
            pe.wait_ge(sum_add, ADDS_PER_NORM * q + need)
            nc.tensor.matmul(total_bank(q, tb)[:, 0:TB[tb][1]], ones[:, :], acc2[q % 2][:, cols(tb)], start=True, stop=True).then_inc(sum_mm, 1)

        pe.wait_ge(const_in, 16 * 10)
        nc.tensor.transpose(bank[5][:, 0:68], rows[0:68, :], ident[0:68, 0:68]).then_inc(vec_mm, 1)
        nc.tensor.transpose(bank[4][:, 0:2 * NMOD], ada_rows[0:2 * NMOD, :], ident[0:2 * NMOD, 0:2 * NMOD]).then_inc(vec_mm, 1)
        pe.wait_ge(fill_ok, 2)
        for tb in range(NTB):
            pe.wait_ge(x_loaded[tb], 16)
            n0 = TB[tb][0] // P
            for d in range(DT):
                i = DT * tb + d
                after(pe, xt_ev, i - 3)
                for n in range(TB[tb][1] // P):
                    mm = nc.tensor.transpose(bank[i % 4][:, n * P:(n + 1) * P], xtok[:, n0 + n, d * P:(d + 1) * P], ident)
                mm.then_inc(xt_mm, 1)
            if tb == 0:
                pe.wait_ge(silu_ok, 1)
            for i in range(4 * tb, min(4 * tb + 4, 8)):
                pe.wait_ge(ada0_in[i], 16)
                for f in range(HT):
                    j = HT * i + f
                    ada_mult(lambda k: ada0[i][:, k, f * P:(f + 1) * P], ADA_BANK[:, 2 * j:2 * j + 2], ada0_mm)
            if tb > 0:
                total(0, tb - 1)
        total(0, NTB - 1)

        G, n_ada = 0, 0
        pe.wait_ge(mod_ok, 1)
        for ui, (kind, half, _, tok) in enumerate(IN_UNITS):
            pe.wait_ge(w_lo, ui + 1)
            wH, wL = (r[ui % 2][:, :].rearrange("p (k n) -> p k n", k=DT) for r in (ringH, ringL))
            for g in range(IN_GROUPS[ui]):
                tb = (0 if g < 4 else 1 if g < 8 else 2) if tok else g // HT
                if ui == 0:
                    pe.wait_ge(h_lo, DT * (tb + 1))
                after(pe, in_ev, G - 3)
                for k in range(DT):
                    if tok:
                        ts = slice(g * P, (g + 1) * P)
                        mm = pair_pass(bank[G % 4][:, 0:UC], wH[:, k, :], wL[:, k, :], hH[:, k, ts], hL[:, k, ts],
                                       k == 0, k == DT - 1, weights_moving=True)
                    else:
                        fs = slice((g % HT) * P, (g % HT + 1) * P)
                        mm = pair_pass(bank[G % 4][:, 0:TB[tb][1]], wH[:, k, fs], wL[:, k, fs], hH[:, k, cols(tb)],
                                       hL[:, k, cols(tb)], k == 0, k == DT - 1)
                mm.then_inc(in_mm, 1)
                G += 1
                if kind == "u":
                    i = NTB * HT * half + g
                    pe.wait_ge(v_norm, NT)
                    after(pe, t_ok, i - 1)
                    for n in range(TB[tb][1] // P):
                        ch = TB[tb][0] // P + n
                        gg = HT * half + g % HT
                        mm = nc.tensor.matmul(bank[4 + i % 2][:, n * P:(n + 1) * P], vtok[:, ch, gg * P:(gg + 1) * P],
                                              wsT[:, gg, :], start=True, stop=True)
                    mm.then_inc(sp_mm, 1)
                if n_ada < ADA_IN and g in ((2, 5, 8) if tok else (1, 3, 5)):
                    c0 = 4 * DT + 2 * n_ada
                    ada_tile(n_ada, slice(c0, c0 + 2))
                    n_ada += 1
            if ui == 0:
                pe.wait_ge(ws_in, 32)
                for g in range(4):
                    mm = nc.tensor.transpose(WS_BANK[:, g * P:(g + 1) * P], ws_raw[:, g, :], ident)
                mm.then_inc(ws_mm, 1)
                pe.wait_ge(ws_ev, 1)

        pe.wait_ge(rot_ok, 2 * HEADS)
        pe.wait_ge(in_ev, G)
        pe.wait_ge(mod_ok, 2)

        def keys(s):
            for d in range(2):
                n = RSTEPS[s][d]
                after(pe, kx_ok, 2 * (s - 2) + d + 1)
                for h in range(HEADS):
                    mm = nc.tensor.transpose(bank[2 * (s % 2) + d][:, h * P:(h + 1) * P], qk[:, HEADS + h, n * P:(n + 1) * P],
                                             ident)
                mm.then_inc(kt_mm, 1)

        def key_values(s):
            for d in range(2):
                n = RSTEPS[s][d]
                pe.wait_ge(kx_ok, 2 * s + d + 1)
                after(pe, s_ok, 2 * (s - 2) + d + 1)
                for h in range(HEADS):
                    mm = nc.tensor.matmul(bank[4 + 2 * (s % 2) + d][:, h * P:(h + 1) * P], kx[s % 2][:, d, h, :],
                                          val[:, n, h * P:(h + 1) * P], start=True, stop=True)
                mm.then_inc(kv_mm, 1)

        for s in range(len(RSTEPS) + 1):
            if s < len(RSTEPS):
                keys(s)
            if s > 0:
                key_values(s - 1)
        pe.wait_ge(s_ok, 2 * len(RSTEPS))
        for k in range(NT + 3):
            m = k - 3
            if 0 <= m < NT:
                pe.wait_ge(b_ok, m + 1)
                after(pe, b_lo, m - 1)
                for h in range(HEADS):
                    mm = nc.tensor.transpose(bank[6 + m % 2][:, h * P:(h + 1) * P], yn[m % 2][:, 0, h, :], ident)
                mm.then_inc(bt_mm, 1)
            if k < NT:
                after(pe, pt_ok, 2 * (k - 1))
                for h in range(HEADS):
                    mm = nc.tensor.matmul(bank[k % 2][:, h * P:(h + 1) * P], qk[:, HEADS + h, k * P:(k + 1) * P],
                                          qk[:, h, k * P:(k + 1) * P], start=True, stop=True)
                mm.then_inc(sc_mm, 1)
            n = k - 1
            if 0 <= n < NT:
                for d in range(2):
                    pe.wait_ge(pt_ok, 2 * n + d + 1)
                    pe.wait_ge(qd_ok, 2 * n + d + 1)
                    after(pe, yn_ok, 2 * (n - 2) + d + 1)
                    for h in range(HEADS):
                        out = bank[2 + 2 * (n % 2) + d][:, h * P:(h + 1) * P]
                        nc.tensor.matmul(out, pt[n % 2][:, d, h, :], val[:, n, h * P:(h + 1) * P], start=True, stop=False)
                        mm = nc.tensor.matmul(out, qd[n % 2][:, d, h, :], S[d][:, n, h, :], start=False, stop=True)
                    mm.then_inc(y_mm, 1)

        pe.wait_ge(b_lo, NT)
        G = 0
        for u in range(N_OUT):
            U = U_OUT + u
            pe.wait_ge(w_lo, U + 1)
            wH, wL = (r[U % 2][:, :].rearrange("p (k n) -> p k n", k=DT) for r in (ringH, ringL))
            for g in range(NTB * HT):
                tb, fs = g // HT, slice((g % HT) * P, (g % HT + 1) * P)
                after(pe, out_ev, G - 3)
                order = [4, 5, 6, 7, 0, 1, 2, 3]
                for k in order:
                    if G == 0 and k == 0:
                        pe.wait_ge(a_back, 32)
                    mm = pair_pass(bank[G % 4][:, 0:TB[tb][1]], wH[:, k, fs], wL[:, k, fs], hH[:, k, cols(tb)],
                                   hL[:, k, cols(tb)], k == order[0], k == order[-1])
                mm.then_inc(out_mm, 1)
                G += 1
        for tb in range(NTB):
            total(1, tb)

        def mlp(l, ch, first=False, last=False):
            UA, n0 = U_MLP[l] + 2 * ch, NTB * HT * ch
            sa, sb_ = U_MLP[l] % 2, (U_MLP[l] + 1) % 2
            aH, aL = (r[sa][:, :].rearrange("p (k n) -> p k n", k=DT) for r in (ringH, ringL))
            bH, bL = (r[sb_][:, :].rearrange("p (k n) -> p k n", k=HT) for r in (ringH, ringL))
            pe.wait_ge(w_lo, UA + 1)
            for tb in range(NTB):
                if first:
                    pe.wait_ge(h_lo, GRP * (l + 1) + DT * (tb + 1))
                for f in range(HT):
                    g = HT * tb + f
                    after(pe, relu_ok[l], n0 + g - 1)
                    for k in range(DT):
                        mm = pair_pass(bank[g % 2][:, 0:TB[tb][1]], aH[:, k, f * P:(f + 1) * P], aL[:, k, f * P:(f + 1) * P],
                                       hH[:, k, cols(tb)], hL[:, k, cols(tb)], k == 0, k == DT - 1)
                    mm.then_inc(m1_mm[l], 1)

            def ada(j):
                if l == 0:
                    n = ADA_IN + ADA_PER_CHUNK * ch + j
                    ada_tile(n, slice(2 * (n - ADA_IN), 2 * (n - ADA_IN) + 2) if isinstance(ch, int)
                             else bass.ds(2 * ADA_PER_CHUNK * ch + 2 * j, 2))

            ada(0)
            pe.wait_ge(w_lo, UA + 2)
            for tb in range(NTB):
                pe.wait_ge(mid_lo[l], n0 + HT * (tb + 1))
                for d in range(DT):
                    i = DT * tb + d
                    after(pe, m2_ev[l], GRP * ch + i - 3)
                    for k in range(HT):
                        mm = pair_pass(bank[2 + i % 4][:, 0:TB[tb][1]], bH[:, k, d * P:(d + 1) * P], bL[:, k, d * P:(d + 1) * P],
                                       midH[:, k, cols(tb)], midL[:, k, cols(tb)], k == 0, k == HT - 1)
                    mm.then_inc(m2_mm[l], 1)
                if tb < 2:
                    ada(tb + 1)
                if last and tb > 0:
                    total(2 * l + 2, tb - 1)
            if last:
                total(2 * l + 2, NTB - 1)

        mlp(0, 0, first=True)
        with pe.Fori(1, NCH - 1) as ch:
            mlp(0, ch)
        mlp(0, NCH - 1, last=True)

        pe.wait_ge(w_lo, U_POOL + 1)
        wH, wL = (r[U_POOL % 2][:, :].rearrange("p (k n) -> p k n", k=DT) for r in (ringH, ringL))
        for i, (tb, d) in enumerate(BY_PAIR):
            g = d // 2
            pe.wait_ge(p_lo, 2 * g + 2)
            after(pe, pool_ev, i - 3)
            fs = slice((d % 2) * P, (d % 2 + 1) * P)
            for k in (2 * g, 2 * g + 1):
                mm = pair_pass(bank[i % 4][:, 0:TB[tb][1]], wH[:, k, fs], wL[:, k, fs], hH[:, k, cols(tb)], hL[:, k, cols(tb)],
                               k == 2 * g, k == 2 * g + 1)
            mm.then_inc(pool_mm, 1)
        for tb in range(NTB):
            total(3, tb)

        mlp(1, 0, first=True)
        with pe.Fori(1, NCH - 1) as ch:
            mlp(1, ch)
        mlp(1, NCH - 1, last=True)
        for n in range(NT):
            tb = 0 if n < 4 else 1 if n < 8 else 2
            pe.wait_ge(yt_ok, DT * (tb + 1))
            for half, ev in ((0, yt_eva), (1, yt_evv)):
                after(pe, ev, n - 1)
                for j in range(4):
                    mm = nc.tensor.transpose(bank[(2 * n + half) % 4][:, j * P:(j + 1) * P], yT[:, 4 * half + j, n * P:(n + 1) * P],
                                             ident)
                mm.then_inc(yt_mm, 1)


_INS = ["x_prompt", "x_sample", "state_ret", "c", "c_ctx", "ada_w", "ada_b", "norm_mix", "norm_mlp", "mlp_w1", "mlp_w2",
        "ev_w_in", "ev_w_s", "ev_b_s", "ev_vnorm", "ev_decay", "ev_w_out", "od_w_pool", "od_pool_scale", "final_norm"]
_OUTS = [((1, PROMPT, D), "float32"), ((1, SAMPLE, D), "float32"), ((1, 1, 2, HEADS, P, P), "float32")]


def constants():
    j = np.arange(P, dtype=np.float32)
    small = np.ones((P, P + 2 + 64), np.float32)
    small[:, 0:P] = np.eye(P, dtype=np.float32)
    small[:, P] = P - 1 - j
    small[:, P + 1] = j
    for g, w in enumerate(WINDOWS):
        for e in range(PADW):
            small[:, P + 2 + 16 * g + e] = w / min(w, e + w // 2)
            small[:, P + 2 + 16 * g + 8 + e] = w / min(w, PADW - e + w // 2)
    rows, cs = np.meshgrid(j, j, indexing="ij")
    pos = np.stack([np.maximum(cs - rows, 0), np.maximum(rows - cs, 0), cs + 1, P - cs], axis=1).astype(np.float32)
    pos = np.repeat(pos[:, :, None, :], HEADS, axis=2).reshape(P, 4 * HEADS * P)
    pairs = P // 4
    inv = np.float32(10000.0) ** (-np.arange(pairs, dtype=np.float32) / np.float32(pairs))
    t = np.arange(SAMPLE)
    ang = np.concatenate([np.float32(t // GRID_W)[:, None] * inv, np.float32(t % GRID_W)[:, None] * inv], axis=1).T
    ang = ang.astype(np.float32)
    cos, sin = np.cos(ang), np.sin(ang)
    rope = np.stack([np.concatenate([cos, cos]), np.concatenate([-sin, sin])], axis=1).astype(np.float32)
    return {"small_const": small, "pos_const": pos, "rope_const": rope}


def kernel(**inputs):
    from contextlib import ExitStack
    import concourse.bacc as _bacc
    from concourse.bass_utils import run_bass_kernel_spmd as _run

    nc = _bacc.Bacc("TRN2", target_bir_lowering=False, num_devices=1, dynamic_dma_scratch_size=1024)
    arrays, args = {}, []
    for name, a in [(n, inputs[n]) for n in _INS] + list(constants().items()):
        a = np.ascontiguousarray(a)
        arrays[f"in_{name}_dram"] = a
        args.append(nc.dram_tensor(f"in_{name}_dram", a.shape, mybir.dt.from_np(a.dtype), kind="ExternalInput").ap())
    for i, (shape, dtype) in enumerate(_OUTS):
        args.append(nc.dram_tensor(f"out_{i}_dram", shape, mybir.dt.from_np(np.dtype(dtype)), kind="ExternalOutput").ap())
    with ExitStack() as ctx:
        build(nc, ctx, *args)
    r = _run(nc, [arrays], core_ids=[0])
    return tuple(r.results[0][f"out_{i}_dram"] for i in range(len(_OUTS)))
```

```python
import numpy as np
import concourse.bass as bass
from concourse import mybir

F32 = mybir.dt.float32
F32R = mybir.dt.float32r
ALU = mybir.AluOpType
ACT = mybir.ActivationFunctionType

P = 128
D = 1024
DT = D // P
SAMPLE, PROMPT = 1024, 256
T = SAMPLE + PROMPT
NT = T // P
NS = SAMPLE // P
HEADS = 4
HW = HEADS * P
F = 4096
UC = 256
NCH = F // UC
HT = UC // P
NMOD = 6 * DT
EPS = 1e-6
WINDOWS = (2, 4, 8, 16)
PADW = 8
PW = SAMPLE + PROMPT + 4 * PADW
TB = [(0, 512, 1), (512, 512, 1), (1024, 256, 0)]
NTB = len(TB)
GRP = NTB * DT
GRID_W = 64

IN_UNITS = ([("v", i, 512 + i * UC, True) for i in range(2)] + [("q", 0, 1024, False)]
            + [("u", i, i * UC, False) for i in range(2)] + [("q", 1, 1024 + UC, False)]
            + [("k", i, 1536 + i * UC, False) for i in range(2)]
            + [("val", i, 2048 + i * UC, True) for i in range(2)] + [("gf", i, 2560 + i * UC, True) for i in range(2)]
            + [("gb", i, 3072 + i * UC, True) for i in range(2)])
N_IN = len(IN_UNITS)
U_OUT = N_IN
N_OUT = D // UC
U_MLP = [U_OUT + N_OUT, U_OUT + N_OUT + 2 * NCH + 1]
U_POOL = U_MLP[1] - 1
IN_GROUPS = [NT if tok else NTB * HT for _, _, _, tok in IN_UNITS]
IN_CUM = [sum(IN_GROUPS[:i]) for i in range(N_IN + 1)]
ADA_BATCH = NMOD // NCH
ADA_IN_UNITS = {0: 0, 3: 1, 4: 2, 5: 3, 6: 4, 7: 5, 8: 6, 9: 7}
ADA_IN = ADA_BATCH * len(ADA_IN_UNITS)
ADA_L0 = NMOD - 2 * DT
ADA_OUT_TILES = [range(n, min(n + ADA_BATCH, ADA_L0)) for n in range(ADA_IN, ADA_L0, ADA_BATCH)]
OUT_AT = {i: ADA_IN + n for n, i in enumerate([2, 4, 7, 9, 12, 14, 17, 19])}
OUT_TOTAL_AT = {9: 0, 16: 1, 22: 2}
BATCHES_IN = len(ADA_IN_UNITS)
BATCHES_L0 = BATCHES_IN + len(ADA_OUT_TILES)

BY_BLOCK = [(t, d) for t in range(NTB) for d in range(DT)]
BY_PAIR = [(t, HT * u + f) for u in range(DT // HT) for t in range(NTB) for f in range(HT)]
POOL_TILES = [6, 7, 4, 5, 2, 3, 0, 1]
BY_POOL = [(t, d + f) for d in POOL_TILES[::HT] for t in range(NTB) for f in range(HT)]
PAIRS = NTB * HT
NORM_ORDER = [BY_BLOCK, BY_PAIR, BY_BLOCK, BY_POOL, BY_BLOCK]


def add_numbers(order):
    out, n = {}, 0
    for t, d in order:
        if d == 0:
            out[(t, d)] = None
        else:
            out[(t, d)] = n
            n += 1
    return out


ADDS = [add_numbers(o) for o in NORM_ORDER]
ADDS_PER_NORM = GRP - NTB
ADD_BASE = [ADDS_PER_NORM * n for n in (0, 1, 2, 3, 3)]
SUM_BASE = [NTB * n for n in (0, 1, 2, 3, 3)]

RSTEPS = [(s, NS - 1 - s) for s in range(NS)] + [(NS, NS + 1), (NS + 1, NS)]
ADVANCE = [s for s in range(NT) if s != NS - 1]
R_UNITS = {11: range(0, 4), 12: range(4, 7), 13: range(7, 10)}


def advances_before(s):
    return sum(1 for a in ADVANCE if a < s)


def after(eng, sem, n):
    if isinstance(n, int) and n <= 0:
        return
    eng.wait_ge(sem, n)


def build(nc, ctx, x_prompt, x_sample, state_ret, c, c_ctx, ada_w, ada_b, norm_mix, norm_mlp, mlp_w1, mlp_w2,
          ev_w_in, ev_w_s, ev_b_s, ev_vnorm, ev_decay, ev_w_out, od_w_pool, od_pool_scale, final_norm,
          small_const, pos_const, rope_const, y_prompt, y_sample, new_state):
    KB = 1024
    base = (nc.sbuf_base + 31) // 32 * 32

    def at(name, kb, shape, dt=F32):
        return nc.alloc_sbuf_tensor_at(name, shape, dt, offset=base + int(kb * KB))

    A_H, A_L, A_X, A_M, A_E, A_R0, A_R1, A_ST, A_AD, A_C = 0, 40, 80, 120, 140, 160, 176, 192, 200, 204
    hH = at("hH", A_H, [P, DT, T], F32R)
    hL = at("hL", A_L, [P, DT, T], F32R)
    X = at("X", A_X, [P, DT, T])
    midH = at("midH", A_M, [P, HT, T], F32R)
    midL = at("midL", A_M + 10, [P, HT, T], F32R)
    ringH = [at(f"ringH{i}", a, [P, 2048], F32R) for i, a in enumerate((A_R0, A_R1))]
    ringL = [at(f"ringL{i}", a + 8, [P, 2048], F32R) for i, a in enumerate((A_R0, A_R1))]
    stage = at("stage", A_ST, [P, 2048])
    ada_st = at("ada_st", A_AD, [P, DT, P])
    xn_b = [at(f"xn{i}", A_E + 2 * i, [P, 512]) for i in range(2)]
    hs_b = [at(f"hs{i}", A_E + 4 + 2 * i, [P, 512]) for i in range(2)]
    sq_b = [at(f"sq{i}", A_E + 11 + 2 * i, [P, 512]) for i in range(2)]
    xtok = at("xtok", A_H, [P, NT, D])
    ada0 = [at(f"ada0_{i}", a, [P, DT, UC]) for i, a in enumerate([A_L + 8 * j for j in range(5)]
                                                                   + [A_M, A_M + 8, A_R1])]
    xnT = at("xnT", A_H, [P, DT, T])
    rows = at("rows", A_R1 + 8, [P, P])
    ada_rows = at("ada_rows", A_R1 + 8.5, [P, P])
    mod_rows = at("mod_rows", A_E, [2, 2 * DT * P])
    vtok = at("vtok", A_M, [P, NT, 512])
    ug = [at(f"ug{i}", A_E + 2 * i, [P, 512]) for i in range(2)]
    ws_raw = at("ws_raw", A_E, [P, 4, P])
    ga = [at(f"ga{i}", A_E + 4 + 2 * i, [P, 512]) for i in range(2)]
    gaH = [at(f"gaH{i}", A_E + 8 + 2 * i, [P, 512], F32R) for i in range(2)]
    gaL = [at(f"gaL{i}", A_E + 12 + 2 * i, [P, 512], F32R) for i in range(2)]
    bias_b = at("bias_b", A_E + 16, [P, 4, P])
    wsT = at("wsT", A_E + 18, [P, 4, P])
    qk = at("qk", A_X, [P, 2 * HEADS, T])
    rope = at("rope", A_M, [P, 2, SAMPLE])
    swap = [at(f"swap{i}", A_M + 8 + 4 * i, [P, SAMPLE]) for i in range(2)]
    val = at("val", A_E, [P, NT, HW])
    gate_st = at("gate_st", A_M, [P, NT, UC])
    tab = at("tab", A_M + 10, [P, 4, HEADS, P])
    pt = [at(f"pt{i}", A_M + 4 * i, [P, 2, HEADS, P]) for i in range(2)]
    qd = [at(f"qd{i}", A_R1 + 4 * i, [P, 2, HEADS, P]) for i in range(2)]
    yn = [at(f"yn{i}", A_R1 + 8 + 4 * i, [P, 2, HEADS, P]) for i in range(2)]
    prow = [[at(f"prow{i}_{j}", A_M + (3 * i + j) * PW * 4 / KB, [P, PW]) for j in range(3)] for i in range(2)]
    yT = at("yT", A_H, [P, DT, T])
    ytok = at("ytok", A_L, [P, NT, D])

    off = [A_C]

    def small(name, shape):
        n = int(np.prod(shape[1:])) * 4
        t = at(name, off[0], shape)
        off[0] += ((n + 31) // 32 * 32) / KB
        return t

    csm = small("csm", [P, P + 2 + 64])
    ident = csm[:, 0:P]
    edges = csm[:, P + 2:P + 66].rearrange("p (g s e) -> p g s e", g=4, s=2)
    vec = small("vec", [P, 68])
    adab = small("adab", [P, 2 * NMOD])
    sc2 = small("sc2", [P, DT, 2])
    mod = small("mod", [P, 2, NMOD, 2])
    gain = [small(f"gain{q}", [P, DT, 2]) for q in range(4)]
    gpool = small("gpool", [P, DT, 2])
    eps_t = small("eps_t", [P, 1])
    dec = small("dec", [P, 8])
    ned = small("ned", [P, 8])
    kd = small("kd", [P, 8])
    cd = small("cd", [P, 8])
    vmv = small("vmv", [P, NT * 4, 2])
    vst = small("vst", [P, NT * 4, 6])
    rst = [small(f"rst{i}", [P, 8, 6]) for i in range(2)]
    rmv = [small(f"rmv{i}", [P, 8, 2]) for i in range(2)]
    rnm = [small(f"rnm{i}", [P, 8]) for i in range(2)]
    ones = small("ones", [P, P])
    ones_r = at("ones_r", off[0], [P, 8], F32R)
    off[0] += 32 / KB
    A_V = off[0]
    r_b = [at(f"relu{i}", A_V + 2 * i, [P, 512]) for i in range(3)]
    acc2 = [at("acc0", A_E + 15, [P, T]), at("acc1", A_V + 6, [P, T])]
    ada_pr = [at("ada_pr_in", A_V, [P, DT, P]), at("ada_pr_mlp", A_E, [P, DT, P])]
    ada_sum = [at("ada_sum_in", A_V + 4, [P, ADA_BATCH, 2, P]), at("ada_sum_mlp", A_E + 8, [P, ADA_BATCH, 2, P])]
    ada_sH = [at("ada_sh_in", A_V + 7, [P, ADA_BATCH, 2, P], F32R), at("ada_sh_mlp", A_E + 4, [P, ADA_BATCH, 2, P], F32R)]
    ada_sL = [at("ada_sl_in", A_V + 10, [P, ADA_BATCH, 2, P], F32R), at("ada_sl_mlp", A_E + 8, [P, ADA_BATCH, 2, P], F32R)]
    kx = [at(f"kx{i}", A_V + 4 * i, [P, 2, HEADS, P]) for i in range(2)]
    gt = [at(f"gt{i}", A_V + 4 * i, [P, 2, 2, UC]) for i in range(2)]
    S = [[at("SF0", A_AD, [P, HEADS, P]), at("SF1", A_AD + 2, [P, HEADS, P])],
         [at("SB0", A_M + 18, [P, HEADS, P]), at("SB1", A_V + 8, [P, HEADS, P])]]
    assert base + (A_V + 13) * KB <= nc.sbuf_usable_end, (base + (A_V + 13) * KB, nc.sbuf_usable_end)

    bank = [nc.alloc_psum_tensor(f"bank{i}", [P, 512], F32) for i in range(8)]
    ADA_BANK, WS_BANK = bank[7], bank[6]
    ADA_COL0 = 4 * DT

    x_dram = nc.dram_tensor("x_spill", [P, DT, T], F32, kind="Internal").ap()
    a_dram = nc.dram_tensor("a_spill", [2, P, HEADS, T], F32, kind="Internal").ap()
    s_dram = nc.dram_tensor("state_spill", [2, NT, P, HEADS * P], F32, kind="Internal").ap()
    g_dram = nc.dram_tensor("gate_spill", [4, P, NT, UC], F32, kind="Internal").ap()

    ada_v = [ada_w[l].rearrange("(k p) f -> p k f", p=P) for l in range(2)]
    win_v = ev_w_in[0].rearrange("(k p) f -> p k f", p=P)
    wout_v = ev_w_out[0].rearrange("(k p) f -> p k f", p=P)
    w1_v = [mlp_w1[l].rearrange("(k p) f -> p k f", p=P) for l in range(2)]
    w2_v = [mlp_w2[l].rearrange("(k p) d -> p k d", p=P) for l in range(2)]
    wpool_v = od_w_pool[0].rearrange("g (k p) d -> p (g k) d", p=P)
    x_in = [x_sample[0, 0:512].rearrange("(n p) d -> p n d", p=P),
            x_sample[0, 512:1024].rearrange("(n p) d -> p n d", p=P),
            x_prompt[0].rearrange("(n p) d -> p n d", p=P)]
    y_out = [y_sample[0, n * P:(n + 1) * P, :] for n in range(NS)] + [y_prompt[0, n * P:(n + 1) * P, :] for n in range(2)]

    def sem(name, n=None):
        return nc.alloc_semaphore(name) if n is None else [nc.alloc_semaphore(f"{name}{i}") for i in range(n)]

    const_in, ones_ok, x_loaded, ada0_in = sem("const_in"), sem("ones_ok"), sem("x_loaded", NTB), sem("ada0_in", 8)
    fill_ok, vec_mm, vec_ev, silu_ok = sem("fill_ok"), sem("vec_mm"), sem("vec_ev"), sem("silu_ok")
    dec_exp, dec_neg, dec_tab = sem("dec_exp"), sem("dec_neg"), sem("dec_tab")
    xt_mm, xt_ev, x_spilled, ada0_mm, mod_ok, gain_ok = (sem("xt_mm"), sem("xt_ev"), sem("x_spilled"), sem("ada0_mm"),
                                                         sem("mod_ok"), sem("gain_ok"))
    xn_v, row_ok, row_mm, a_shi, a_slo = sem("xn_v"), sem("row_ok"), sem("row_mm"), sem("a_shi"), sem("a_slo")
    w_raw, w_hi, w_lo, a_raw, a_mm = sem("w_raw"), sem("w_hi"), sem("w_lo"), sem("a_raw"), sem("a_mm")
    sq_mm = sem("sq_mm")
    sq_ok, sum_add, sum_mm, rms_ok, rstd_ok = sem("sq_ok"), sem("sum_add"), sem("sum_mm"), sem("rms_ok"), sem("rstd_ok")
    xn_ok, hs_ok, h_hi, h_lo = sem("xn_ok"), sem("hs_ok"), sem("h_hi"), sem("h_lo")
    in_mm, in_ev, ws_in, ws_mm, ws_ev = sem("in_mm"), sem("in_ev"), sem("ws_in"), sem("ws_mm"), sem("ws_ev")
    v_bn, v_stat, v_sd, v_rstd, v_norm = sem("v_bn"), sem("v_stat"), sem("v_sd"), sem("v_rstd"), sem("v_norm")
    sp_mm, t_ok, a_ok, a_hi, a_lo, a_spilled = (sem("sp_mm"), sem("t_ok"), sem("a_ok"), sem("a_hi"), sem("a_lo"),
                                                sem("a_spilled", 2))
    rope_in, swap_in, rot_s, rot_c, rot_ok, gate_out = (sem("rope_in"), sem("swap_in", 2), sem("rot_s"), sem("rot_c"),
                                                        sem("rot_ok"), sem("gate_out"))
    pos_in, tab_exp, tab_ok, state_in, zero_ok = sem("pos_in"), sem("tab_exp"), sem("tab_ok"), sem("state_in"), sem("zero_ok")
    s_out, s_back, a_pr, a_sum = sem("s_out", 2), sem("s_back", 2), sem("a_pr"), sem("a_sum")
    kt_mm, kx_ok, kv_mm, s_ok, new_out = sem("kt_mm"), sem("kx_ok"), sem("kv_mm"), sem("s_ok"), sem("new_out")
    sc_mm, pt_ok, qd_ok, y_mm, y_bn, y_stat = sem("sc_mm"), sem("pt_ok"), sem("qd_ok"), sem("y_mm"), sem("y_bn"), sem("y_stat")
    y_sd, y_rstd, y_nmr, yn_ok, gate_in = sem("y_sd"), sem("y_rstd"), sem("y_nmr"), sem("yn_ok"), sem("gate_in", 2)
    gm_f, gm_b, b_ok, bt_mm, b_hi, b_lo = sem("gm_f"), sem("gm_b"), sem("b_ok"), sem("bt_mm"), sem("b_hi"), sem("b_lo")
    x_back, a_back, out_mm, out_ev = sem("x_back", NTB), sem("a_back"), sem("out_mm"), sem("out_ev")
    pz_ok, pxn, ph, pw, pe_ok, pp = sem("pz_ok"), sem("pxn"), sem("ph"), sem("pw"), sem("pe_ok"), sem("pp")
    p_hi, p_lo, pool_mm, pool_ev = sem("p_hi"), sem("p_lo"), sem("pool_mm"), sem("pool_ev")
    m1_mm, relu_ok, sqr_ok, mid_hi, mid_lo = (sem("m1_mm", 2), sem("relu_ok", 2), sem("sqr_ok", 2), sem("mid_hi", 2),
                                              sem("mid_lo", 2))
    m2_mm, m2_ev = sem("m2_mm", 2), sem("m2_ev", 2)
    yt_ok, yt_mm, yt_eva, yt_evv, y_done = sem("yt_ok"), sem("yt_mm"), sem("yt_eva"), sem("yt_evv"), sem("y_done")

    def cols(tb):
        t0, w, _ = TB[tb]
        return slice(t0, t0 + w)

    def pair_pass(out, w_hi_ap, w_lo_ap, m_hi_ap, m_lo_ap, first, last, weights_moving=False):
        if weights_moving:
            terms = ((m_hi_ap, w_hi_ap), (m_hi_ap, w_lo_ap), (m_lo_ap, w_hi_ap))
        else:
            terms = ((w_hi_ap, m_hi_ap), (w_hi_ap, m_lo_ap), (w_lo_ap, m_hi_ap))
        for n, (a, b) in enumerate(terms):
            mm = nc.tensor.matmul(out, a, b, start=first and n == 0, stop=last and n == 2)
        return mm

    X_READY = [(xt_ev, 0), (out_ev, 0), (m2_ev[0], GRP * (NCH - 1)), (pool_ev, 0), (m2_ev[1], GRP * (NCH - 1))]
    TURN = {0: 0, 1: 1, 3: 2}

    def total_bank(q, tb):
        return (bank[6], bank[5], bank[4])[tb] if q in TURN else (bank[6], bank[0], bank[1])[tb]

    def shift(q, d, cond):
        return mod[:, q // 2, 3 * DT * (q % 2) + d, cond:cond + 1]

    def pool_dst(d):
        return 1 + (d // 2) % 2

    def xn_done(tb, d):
        return ((xn_ok, xn_v)[d % 2], 4 * tb + d // 2 + 1)

    def xn_total(q):
        return 0 if q == 0 else GRP // 2 + GRP * (TURN[q] - 1)

    def slot_free(U):
        if U < 2:
            return (ada0_mm, 8)
        if U <= U_OUT + 1:
            return (in_mm, IN_CUM[U - 1])
        if U <= U_MLP[0] + 1:
            return (out_mm, NTB * HT * (U - 2 - U_OUT + 1))
        if U == U_POOL:
            return (m1_mm[0], NTB * HT * NCH)
        if U == U_POOL + 1:
            return (m2_mm[0], GRP * NCH)
        return (pool_mm, GRP)

    block = ctx.enter_context(nc.Block())

    @block.sync
    def _(sp):
        def raw(U, view, split=DT):
            after(sp, w_lo, U)
            sp.dma_start(stage[:, :].rearrange("p (k n) -> p k n", k=split), view).then_inc(w_raw, 16)

        def raw_static(U):
            if U < U_OUT:
                raw(U, win_v[:, :, IN_UNITS[U][2]:IN_UNITS[U][2] + UC])
            elif U < U_MLP[0]:
                raw(U, wout_v[:, :, (U - U_OUT) * UC:(U - U_OUT + 1) * UC])
            elif U == U_POOL:
                raw(U, wpool_v)
            else:
                l = 1 if U > U_POOL else 0
                raw_mlp(l, (U - U_MLP[l]) // 2, (U - U_MLP[l]) % 2)

        def raw_mlp(l, ch, second):
            U = U_MLP[l] + 2 * ch + second
            if second:
                raw(U, w2_v[l][:, bass.ds(ch * HT, HT), :], HT)
            else:
                raw(U, w1_v[l][:, :, bass.ds(ch * UC, UC)])

        def ada_tile(n, l, col):
            after(sp, a_sum, n)
            sp.dma_start(ada_st[:, :, :], ada_v[l][:, :, bass.ds(col, P)]).then_inc(a_raw, 16)

        for tb in range(NTB):
            n0, n1 = TB[tb][0] // P, (TB[tb][0] + TB[tb][1]) // P
            sp.dma_start(xtok[:, n0:n1, :], x_in[tb]).then_inc(x_loaded[tb], 16)
            if tb == 0:
                sp.wait_ge(const_in, 16 * 10)
        for i in range(8):
            sp.dma_start(ada0[i][:, :, :], ada_v[0][:, :, i * UC:(i + 1) * UC]).then_inc(ada0_in[i], 16)
        raw_static(0)
        raw_static(1)
        sp.wait_ge(xt_ev, GRP)
        sp.dma_start(x_dram, X[:, :, :]).then_inc(x_spilled, 16)
        def ada_l0(n):
            ada_tile(n, 0, (2 * DT + n) * P)

        for v in range(N_IN):
            is_u = IN_UNITS[v][0] == "u"
            n_ada = ADA_BATCH * ADA_IN_UNITS.get(v, 0)
            if v in ADA_IN_UNITS:
                ada_l0(n_ada)
            if v + 2 <= U_OUT:
                raw_static(v + 2)
            if v == 0:
                sp.wait_ge(h_lo, GRP)
                sp.dma_start(ws_raw[:, :, :], ev_w_s[0].rearrange("g i j -> i g j")).then_inc(ws_in, 16)
                sp.dma_start(bias_b[:, :, :].rearrange("p g i -> p (g i)"),
                             ev_b_s.rearrange("o g i -> o (g i)").to_broadcast([P, 4 * P])).then_inc(ws_in, 16)
            if v in ADA_IN_UNITS and not is_u:
                ada_l0(n_ada + 1)
                ada_l0(n_ada + 2)
            if is_u:
                for tb in range(NTB):
                    if tb > 0:
                        ada_l0(n_ada + tb)
                    for f in range(HT):
                        i = (IN_UNITS[v][1] * NTB + tb) * HT + f
                        g, w = HT * IN_UNITS[v][1] + f, TB[tb][1]
                        sp.wait_ge(a_hi, i + 1)
                        sp.dma_start(a_dram[0][:, g, cols(tb)], gaH[i % 2][:, 0:w].bitcast(F32)).then_inc(a_spilled[i % 2], 16)
                        sp.wait_ge(a_lo, i + 1)
                        sp.dma_start(a_dram[1][:, g, cols(tb)], gaL[i % 2][:, 0:w].bitcast(F32)).then_inc(a_spilled[i % 2], 16)
                if IN_UNITS[v][1] == 1:
                    sp.wait_ge(sp_mm, 2 * NTB * HT)
                    sp.dma_start(rope[:, :, :], rope_const).then_inc(rope_in, 16)
            if v == 8:
                sp.wait_ge(rot_ok, 2 * HEADS)
                sp.dma_start(tab[:, :, :, :].rearrange("p a h i -> p (a h i)"), pos_const).then_inc(pos_in, 16)
            if v == 10:
                sp.wait_ge(a_sum, ADA_IN)
                for d in range(2):
                    sp.dma_start(S[d][0][:, :, :], state_ret[0, 0, d].rearrange("h d e -> d h e")).then_inc(state_in, 16)
            for st in R_UNITS.get(v, ()):
                for d in range(2):
                    n, b = RSTEPS[st][d], st % 2
                    if st == 0:
                        sp.wait_ge(state_in, 32)
                    elif st == NS:
                        sp.wait_ge(zero_ok, d + 1)
                    else:
                        sp.wait_ge(s_ok, 2 * advances_before(st - 1) + d + 1)
                    sp.dma_start(s_dram[d][n], S[d][b][:, :, :].rearrange("p h e -> p (h e)")).then_inc(s_out[b], 16)
        sp.wait_ge(in_mm, IN_CUM[N_IN])
        sp.wait_ge(a_spilled[0], 16 * 2 * NTB * HT)
        sp.wait_ge(a_spilled[1], 16 * 2 * NTB * HT)
        sp.wait_ge(s_ok, 2 * len(ADVANCE))
        for d in range(2):
            sp.dma_start(new_state[0, 0, d].rearrange("h d e -> d h e"), S[d][NT % 2][:, :, :]).then_inc(new_out, 16)
        sp.wait_ge(s_out[0], 16 * NT)
        sp.wait_ge(s_out[1], 16 * NT)
        sp.wait_ge(new_out, 32)

        def state_loads(k):
            after(sp, y_mm, 2 * (k - 1))
            for d in range(2):
                sp.dma_start(S[d][k % 2][:, :, :].rearrange("p h e -> p (h e)"), s_dram[d][k]).then_inc(s_back[k % 2], 16)

        def gate_loads(k):
            after(sp, gm_f, k - 1)
            after(sp, gm_b, k - 1)
            for d in range(2):
                sp.dma_start(gt[k % 2][:, d, :, :],
                             g_dram[2 * d:2 * d + 2, :, k, :].rearrange("h p n -> p h n")).then_inc(gate_in[k % 2], 16)

        state_loads(0)
        state_loads(1)
        sp.wait_ge(gate_out, 32 * 4)
        gate_loads(0)
        gate_loads(1)
        raw_static(U_OUT + 1)
        sp.wait_ge(x_spilled, 16)
        for k in range(2, NT):
            state_loads(k)
            gate_loads(k)
            part, g = (hH, hL)[k % 2], (k - 2) // 2
            sp.dma_start(part[:, g, :].bitcast(F32), a_dram[k % 2][:, g, :]).then_inc(a_back, 16)
            if k in (6, 7):
                sp.wait_ge(sc_mm, 4)
                sp.wait_ge(qd_ok, 8)
                ds = slice(4 * (k - 6), 4 * (k - 5))
                sp.dma_start(X[:, ds, cols(0)], x_dram[:, ds, cols(0)]).then_inc(x_back[0], 16)
        for tb in (1, 2):
            sp.wait_ge(sc_mm, min(4 * (tb + 1), NT))
            sp.wait_ge(qd_ok, 2 * min(4 * (tb + 1), NT))
            sp.dma_start(X[:, :, cols(tb)], x_dram[:, :, cols(tb)]).then_inc(x_back[tb], 16)
        sp.wait_ge(y_mm, 2 * NT)
        ada_l0(ADA_IN)
        for u in range(N_OUT):
            raw_static(U_OUT + 2 + u)
            for n in range(ADA_IN + 2 * u + 1, min(ADA_IN + 2 * u + 3, ADA_L0)):
                ada_l0(n)

        def mlp0_loads(ch, next0, next1):
            n0 = ADA_L0 + ADA_BATCH * ch
            col = ADA_BATCH * P * ch
            ada_tile(n0, 1, col)
            next0()
            ada_tile(n0 + 1, 1, col + P)
            ada_tile(n0 + 2, 1, col + 2 * P)
            next1()

        with sp.Fori(0, NCH - 1) as ch:
            mlp0_loads(ch, lambda: raw_mlp(0, ch + 1, 0), lambda: raw_mlp(0, ch + 1, 1))
        mlp0_loads(NCH - 1, lambda: raw_static(U_POOL), lambda: raw_static(U_MLP[1]))
        raw_static(U_MLP[1] + 1)
        with sp.Fori(1, NCH) as ch:
            raw_mlp(1, ch, 0)
            raw_mlp(1, ch, 1)
        for n in range(NT):
            sp.wait_ge(yt_eva, n + 1)
            sp.wait_ge(yt_evv, n + 1)
            sp.dma_start(y_out[n], ytok[:, n, :]).then_inc(y_done, 16)
        sp.wait_ge(new_out, 32)
        sp.wait_ge(y_done, 16 * NT)

    @block.scalar
    def _(act):
        def split_hi(U, free, slot):
            act.wait_ge(w_raw, 16 * (U + 1))
            act.wait_ge(*free)
            nc.scalar.activation(ringH[slot][:, :], stage[:, :], ACT.Copy).then_inc(w_hi, 1)

        def split_static(U):
            split_hi(U, slot_free(U), U % 2)

        def square(q, i):
            t, d = NORM_ORDER[q][i]
            add, w = ADDS[q][(t, d)], TB[t][1]
            ready, base_n = X_READY[q]
            act.wait_ge(ready, base_n + i + 1)
            if q == 3:
                after(act, sq_mm, i - 1)
                dst = sq_b[i % 2][:, 0:w]
            elif add is None:
                dst = acc2[q % 2][:, cols(t)]
            else:
                after(act, sum_add, ADD_BASE[q] + add - 1)
                dst = sq_b[add % 2][:, 0:w]
            nc.scalar.activation(dst, X[:, d, cols(t)], ACT.Square).then_inc(sq_ok, 1)

        def rms(q, tb):
            if q == 3:
                act.wait_ge(sq_mm, GRP - PAIRS + HT * (tb + 1))
            else:
                act.wait_ge(sum_mm, SUM_BASE[q] + tb + 1)
            nc.scalar.activation(acc2[q % 2][:, cols(tb)], total_bank(q, tb)[:, 0:TB[tb][1]], ACT.Sqrt, bias=eps_t[:, :],
                                 scale=1.0 / D).then_inc(rms_ok, 1)

        def apply_hi(q, tb):
            w, cond = TB[tb][1:]
            act.wait_ge(gain_ok, (1, 2, 0, 5)[q])
            for d in range(DT):
                i = GRP * TURN[q] + DT * tb + d
                if q > 0 and tb == 0 and d in (2, 5):
                    rms(q, 1 + d // 5)
                if q == 0:
                    act.wait_ge(hs_ok, i + 1)
                    nc.scalar.activation(hH[:, d, cols(tb)], hs_b[i % 2][:, 0:w], ACT.Copy).then_inc(h_hi, 1)
                else:
                    act.wait_ge(xn_ok, xn_total(q) + DT * tb + d + 1)
                    nc.scalar.activation(hH[:, d, cols(tb)], xn_b[i % 2][:, 0:w], ACT.Identity,
                                         scale=gain[q][:, d, cond:cond + 1], bias=shift(q, d, cond)).then_inc(h_hi, 1)

        act.dma_start(csm[:, :], small_const).then_inc(const_in, 16)
        vecs = [(0, c_ctx.rearrange("(k p) -> k p", p=P)), (8, c[0].rearrange("(k p) -> k p", p=P)),
                (16, norm_mix.rearrange("l (k p) -> (l k) p", p=P)), (32, norm_mlp.rearrange("l (k p) -> (l k) p", p=P)),
                (48, final_norm.rearrange("(k p) -> k p", p=P)), (56, od_pool_scale[0].rearrange("(k p) -> k p", p=P)),
                (64, ev_vnorm[0])]
        for r, v in vecs:
            act.dma_start(rows[r:r + v.shape[0], :], v).then_inc(const_in, 16)
        act.dma_start(ada_rows[0:2 * NMOD, :], ada_b.rearrange("l (k p) -> (l k) p", p=P)).then_inc(const_in, 16)
        act.dma_start(dec[:, :], ev_decay.rearrange("o a h -> o (a h)").to_broadcast([P, 8])).then_inc(const_in, 16)
        act.wait_ge(const_in, 16 * 10)
        nc.scalar.activation(dec[:, :], dec[:, :], ACT.Exp).then_inc(dec_exp, 1)
        act.wait_ge(dec_neg, 1)
        nc.scalar.activation(kd[:, 0:4], ned[:, 0:4], ACT.Exp, scale=csm[:, P:P + 1]).then_inc(dec_tab, 1)
        nc.scalar.activation(kd[:, 4:8], ned[:, 4:8], ACT.Exp, scale=csm[:, P + 1:P + 2]).then_inc(dec_tab, 1)
        nc.scalar.activation(cd[:, :], ned[:, :], ACT.Exp, scale=float(P)).then_inc(dec_tab, 1)
        act.wait_ge(vec_ev, 1)
        nc.scalar.activation(sc2[:, :, :].rearrange("p k c -> p c k"), vec[:, 0:16].rearrange("p (c k) -> p c k", c=2),
                             ACT.Silu).then_inc(silu_ok, 1)
        act.wait_ge(fill_ok, 2)
        for i in range(GRP):
            square(0, i)
            if i == 2 * DT - 1:
                rms(0, 0)
        rms(0, 1)
        rms(0, 2)
        for b in range(4):
            act.wait_ge(ada0_mm, 2 * (b + 1))
            nc.scalar.activation(mod_rows[0:2, 512 * b:512 * (b + 1)], bank[b][0:2, :], ACT.Copy).then_inc(row_ok, 1)
            if b == 1:
                act.wait_ge(w_raw, 16)
                nc.scalar.activation(ringH[0][:, :], stage[:, :], ACT.Copy).then_inc(w_hi, 1)

        def swap_halves(hd):
            after(act, rot_ok, hd - 1)
            unit = [(k, h) for k, h, _, _ in IN_UNITS].index(("qk"[hd // HEADS], hd % HEADS // HT))
            act.wait_ge(in_ev, IN_CUM[unit] + HT + hd % HT + 1)
            for a, b in ((0, P // 2), (P // 2, 0)):
                act.dma_start(swap[hd % 2][a:a + P // 2, :], qk[b:b + P // 2, hd, 0:SAMPLE]).then_inc(swap_in[hd % 2], 16)

        G, gates = 0, 0
        for ui, (kind, half, _, tok) in enumerate(IN_UNITS):
            for g in range(IN_GROUPS[ui]):
                if ui == 0 and g in (0, 4, 8):
                    apply_hi(0, g // 4)
                if ui == 10 and g == 1:
                    act.wait_ge(pos_in, 16)
                    for a in range(4):
                        for h in range(HEADS):
                            e = nc.scalar.activation(tab[:, a, h, :], tab[:, a, h, :], ACT.Exp,
                                                     scale=ned[:, 4 * (a % 2) + h:4 * (a % 2) + h + 1])
                    e.then_inc(tab_exp, 1)
                act.wait_ge(in_mm, G + 1)
                if tok:
                    src = bank[G if ui == 0 and g < 8 else G % 4][:, 0:UC]
                    lo, hi = half * UC, (half + 1) * UC
                    if kind == "v":
                        ev = nc.scalar.activation(vtok[:, g, lo:hi], src, ACT.Gelu_apprx_tanh)
                    elif kind == "val":
                        if half == 0 and g == 0:
                            for s in a_spilled:
                                act.wait_ge(s, 16 * 2 * NTB * HT)
                        ev = nc.scalar.activation(val[:, g, lo:hi], src, ACT.Copy)
                    else:
                        if g == 0:
                            act.wait_ge(rot_ok, 2 * HEADS)
                            after(act, gate_out, 32 * gates)
                        ev = nc.scalar.activation(gate_st[:, g, :], src, ACT.Silu)
                else:
                    tb, f = g // HT, g % HT
                    w = TB[tb][1]
                    src = bank[G % 4][:, 0:w]
                    if kind == "u":
                        i = (half * NTB + tb) * HT + f
                        if i == 0:
                            act.wait_ge(ws_ev, 1)
                        after(act, a_ok, i - 1)
                        ev = nc.scalar.activation(ug[i % 2][:, 0:w], src, ACT.Gelu_apprx_tanh)
                    else:
                        if kind == "q" and half == 0 and g == 0:
                            act.wait_ge(x_spilled, 16)
                        hd = (HEADS if kind == "k" else 0) + HT * half + f
                        ev = nc.scalar.activation(qk[:, hd, cols(tb)], src, ACT.Copy,
                                                  scale=float(P) ** -0.5 if kind == "k" else 1.0)
                ev.then_inc(in_ev, 1)
                G += 1
                if kind in "qk" and tb == 1 and hd >= HT:
                    swap_halves(hd)
                if ui == 2 and g == 3:
                    act.wait_ge(v_stat, NT)
                    nc.scalar.activation(vmv[:, :, 1], vmv[:, :, 1], ACT.Sqrt, bias=eps_t[:, :]).then_inc(v_sd, 1)
                if kind in ("gf", "gb") and g % (NT // 2) == NT // 2 - 1:
                    act.wait_ge(in_ev, G)
                    n0 = g + 1 - NT // 2
                    act.dma_start(g_dram[gates][:, n0:g + 1, :], gate_st[:, n0:g + 1, :]).then_inc(gate_out, 16)
                if g == 0:
                    split_static(ui + 1)
            if kind == "u" and half == 1:
                act.wait_ge(sp_mm, 2 * NTB * HT)
                swap_halves(0)
                swap_halves(1)
            if kind in ("gf", "gb"):
                gates += 1

        for k in range(NT + 3):
            m = k - 3
            if 0 <= m < NT:
                act.wait_ge(bt_mm, m + 1)
                nc.scalar.activation(hH[:, HEADS:DT, m * P:(m + 1) * P],
                                     bank[6 + m % 2][:, :].rearrange("p (h i) -> p h i", h=HEADS), ACT.Copy).then_inc(b_hi, 1)
            n = k - 1
            if 0 <= n < NT:
                act.wait_ge(y_stat, n + 1)
                nc.scalar.activation(rmv[n % 2][:, :, 1], rmv[n % 2][:, :, 1], ACT.Sqrt, bias=eps_t[:, :]).then_inc(y_sd, 1)
            if 0 <= n < NT:
                act.wait_ge(y_nmr, n + 1)
                after(act, bt_mm, n - 1)
                for d in range(2):
                    for h in range(HEADS):
                        j = HEADS * d + h
                        ev = nc.scalar.activation(yn[n % 2][:, d, h, :], bank[2 + 2 * (n % 2) + d][:, h * P:(h + 1) * P],
                                                  ACT.Identity, scale=rmv[n % 2][:, j, 1:2], bias=rnm[n % 2][:, j:j + 1])
                    ev.then_inc(yn_ok, 1)

        act.wait_ge(bt_mm, NT)
        split_static(U_OUT + 1)
        for u in range(N_OUT):
            for i in range(NTB * HT * u, NTB * HT * (u + 1)):
                square(1, i)
                if i == GRP - NTB:
                    rms(1, 0)
            if u < N_OUT - 1:
                split_static(U_OUT + 2 + u)

        def mlp(l, ch, first=False, last=False):
            q = 2 * l + 1
            U = U_MLP[l] + 2 * ch
            n0 = NTB * HT * ch

            def hidden_hi(g):
                act.wait_ge(sqr_ok[l], n0 + g + 1)
                if g == 0:
                    after(act, m2_mm[l], GRP * ch)
                act_ = nc.scalar.activation(midH[:, g % HT, cols(g // HT)], r_b[g % 3][:, 0:TB[g // HT][1]], ACT.Copy)
                act_.then_inc(mid_hi[l], 1)

            if first:
                for tb in range(NTB):
                    apply_hi(q, tb)
            for g in range(NTB * HT):
                act.wait_ge(m1_mm[l], n0 + g + 1)
                after(act, mid_lo[l], n0 + g - 2)
                nc.scalar.activation(r_b[g % 3][:, 0:TB[g // HT][1]], bank[g if first and g < 4 else g % 2][:, 0:TB[g // HT][1]],
                                     ACT.Relu).then_inc(relu_ok[l], 1)
                if g == 0:
                    split_hi(U + 1, slot_free(U_MLP[l] + 1) if first else (m2_mm[l], GRP * ch), (U_MLP[l] + 1) % 2)
                if g > 0:
                    hidden_hi(g - 1)
            hidden_hi(NTB * HT - 1)
            if not (l == 1 and last):
                split_hi(U + 2, (m1_mm[l], NTB * HT * (ch + 1)), U_MLP[l] % 2)
            if last:
                for i in range(GRP):
                    square(2 * l + 2, i)
                    if i == 2 * DT - 1:
                        rms(2 * l + 2, 0)
                rms(2 * l + 2, 1)
                rms(2 * l + 2, 2)

        mlp(0, 0, first=True)
        with act.Fori(1, NCH - 1) as ch:
            mlp(0, ch)
        mlp(0, NCH - 1, last=True)

        segs = ((PADW, 0, SAMPLE, 1), (SAMPLE + 3 * PADW, SAMPLE, PROMPT, 0))
        split_static(U_MLP[1])

        def pool_hs(n):
            d = POOL_TILES[n]
            act.wait_ge(pxn, n + 1)
            for p0, t0, w, cond in segs:
                a = prow[n % 2][0][:, p0:p0 + w]
                e = nc.scalar.activation(a, a, ACT.Identity, scale=gain[2][:, d, cond:cond + 1], bias=shift(2, d, cond))
            e.then_inc(ph, 1)

        def pool_hi(n):
            d = POOL_TILES[n]
            act.wait_ge(pp, n + 1)
            for p0, t0, w, cond in segs:
                e = nc.scalar.activation(hH[:, d, t0:t0 + w], prow[n % 2][pool_dst(d)][:, p0:p0 + w], ACT.Copy)
            e.then_inc(p_hi, 1)

        act.wait_ge(gain_ok, 4)
        pool_hs(0)
        for n in range(DT):
            if n + 1 < DT:
                pool_hs(n + 1)
            pool_hi(n)
            if n >= 3 and n % 2 == 1:
                for i in range(PAIRS * (n // 2 - 1), PAIRS * (n // 2)):
                    square(3, i)
        for i in range(GRP - PAIRS, GRP):
            square(3, i)
            if i == GRP - NTB:
                rms(3, 0)

        mlp(1, 0, first=True)
        with act.Fori(1, NCH - 1) as ch:
            mlp(1, ch)
        mlp(1, NCH - 1, last=True)
        for n in range(NT):
            act.wait_ge(yt_mm, 2 * n + 1)
            nc.scalar.activation(ytok[:, n, 0:512], bank[(2 * n) % 4][:, :], ACT.Copy).then_inc(yt_eva, 1)

    @block.gpsimd
    def _(pool):
        def split_lo(U, slot=None):
            slot = U % 2 if slot is None else slot
            pool.wait_ge(w_hi, U + 1)
            nc.gpsimd.tensor_tensor(ringL[slot][:, :], stage[:, :], ringH[slot][:, :].bitcast(F32),
                                    ALU.subtract).then_inc(w_lo, 1)

        def add_square(q, i):
            t, d = NORM_ORDER[q][i]
            add = ADDS[q][(t, d)]
            if add is None:
                return
            pool.wait_ge(sq_ok, GRP * q + i + 1)
            after(pool, sum_add, ADD_BASE[q] + add)
            acc = acc2[q % 2][:, cols(t)]
            nc.gpsimd.tensor_tensor(acc, acc, sq_b[add % 2][:, 0:TB[t][1]], ALU.add).then_inc(sum_add, 1)

        def apply_xn(q, tb):
            pool.wait_ge(rstd_ok, NTB * q + tb + 1)
            for d in range(DT):
                i = GRP * TURN[q] + DT * tb + d
                after(pool, h_lo, i - 1)
                nc.gpsimd.tensor_tensor(xn_b[i % 2][:, 0:TB[tb][1]], X[:, d, cols(tb)], acc2[q % 2][:, cols(tb)],
                                        ALU.mult).then_inc(xn_ok, 1)

        def ada_product(n, pr):
            pool.wait_ge(a_raw, 16 * (n + 1))
            pool.wait_ge(silu_ok, 1)
            c0, c1 = (sc2[:, :, i].unsqueeze(2).to_broadcast([P, DT, P]) for i in range(2))
            nc.gpsimd.tensor_tensor(ada_pr[pr][:, :, :], ada_st[:, :, :], c0, ALU.mult).then_inc(a_pr, 1)
            nc.gpsimd.tensor_tensor(ada_st[:, :, :], ada_st[:, :, :], c1, ALU.mult).then_inc(a_pr, 1)

        nc.gpsimd.memset(ones[:, :], 1.0).then_inc(fill_ok, 1)
        nc.gpsimd.memset(eps_t[:, :], EPS).then_inc(fill_ok, 1)

        def start_xn(tb):
            pool.wait_ge(rstd_ok, tb + 1)
            for d in range(0, DT, 2):
                nc.gpsimd.tensor_tensor(xnT[:, d, cols(tb)], X[:, d, cols(tb)], acc2[0][:, cols(tb)], ALU.mult).then_inc(xn_ok, 1)

        for i in range(GRP):
            add_square(0, i)
        pool.wait_ge(xt_mm, GRP)
        for tb in range(NTB):
            start_xn(tb)
        split_lo(0)
        def rotate_cos(hd):
            pool.wait_ge(rope_in, 16)
            pool.wait_ge(swap_in[hd % 2], 32 * (hd // 2 + 1))
            nc.gpsimd.tensor_tensor(qk[:, hd, 0:SAMPLE], qk[:, hd, 0:SAMPLE], rope[:, 0, :], ALU.mult).then_inc(rot_c, 1)

        for ui, (kind, half, _, tok) in enumerate(IN_UNITS):
            split_lo(ui + 1)
            n_ada = ADA_BATCH * ADA_IN_UNITS.get(ui, 0)
            if ui in ADA_IN_UNITS and kind != "u":
                for j in range(ADA_BATCH):
                    ada_product(n_ada + j, 0)
            if kind == "u":
                for g in range(NTB * HT):
                    i, w = NTB * HT * half + g, TB[g // HT][1]
                    pool.wait_ge(a_ok, i + 1)
                    after(pool, a_spilled[i % 2], 32 * (i // 2))
                    nc.gpsimd.tensor_copy(gaH[i % 2][:, 0:w], ga[i % 2][:, 0:w]).then_inc(a_hi, 1)
                    pool.wait_ge(a_hi, i + 1)
                    nc.gpsimd.tensor_tensor(gaL[i % 2][:, 0:w], ga[i % 2][:, 0:w], gaH[i % 2][:, 0:w].bitcast(F32),
                                            ALU.subtract).then_inc(a_lo, 1)
                    if g % 2 == 1:
                        ada_product(n_ada + g // 2, 0)
            if kind in "qk" and ui > 2 or kind == "u" and half == 1:
                h0 = 0 if kind == "u" else (HEADS if kind == "k" else 0) + HT * half
                rotate_cos(h0)
                rotate_cos(h0 + 1)
            if ui == 10:
                pool.wait_ge(tab_exp, 1)
                for a, sign in ((0, 1), (1, -1)):
                    nc.gpsimd.affine_select(out=tab[:, a, :, :], in_=tab[:, a, :, :], compare_op=ALU.is_ge, fill=0.0,
                                            base=0, pattern=[[0, HEADS], [sign, P]], channel_multiplier=-sign).then_inc(tab_ok, 1)
            if ui == 13:
                for d in range(2):
                    pool.wait_ge(s_ok, 2 * advances_before(NS - 1))
                    pool.wait_ge(s_out[0], 16 * NS)
                    nc.gpsimd.memset(S[d][NS % 2][:, :, :], 0.0).then_inc(zero_ok, 1)
        pool.wait_ge(tab_ok, 2)
        pool.wait_ge(in_mm, IN_CUM[N_IN])
        for k in range(NT + 2):
            if k < NT:
                after(pool, y_mm, 2 * (k - 1))
                for d in range(2):
                    nc.gpsimd.tensor_tensor(qd[k % 2][:, d, :, :], qk[:, 0:HEADS, k * P:(k + 1) * P], tab[:, 2 + d, :, :],
                                            ALU.mult).then_inc(qd_ok, 1)
            n = k - 2
            if n >= 0:
                pool.wait_ge(yn_ok, 2 * n + 2)
                pool.wait_ge(gate_in[n % 2], 32 * (n // 2 + 1))
                y0, y1 = (yn[n % 2][:, d, :, :].rearrange("p h e -> p (h e)") for d in range(2))
                nc.gpsimd.tensor_tensor(y1, y1, gt[n % 2][:, 1, :, :].rearrange("p a n -> p (a n)"), ALU.mult).then_inc(gm_b, 1)
                pool.wait_ge(gm_b, n + 1)
                pool.wait_ge(gm_f, n + 1)
                nc.gpsimd.tensor_tensor(y0, y0, y1, ALU.add).then_inc(b_ok, 1)
        split_lo(U_OUT + 1)
        pool.wait_ge(y_mm, 2 * NT)
        for u in range(N_OUT):
            for i in range(NTB * HT * u, NTB * HT * (u + 1)):
                add_square(1, i)
                if i + 1 in OUT_AT:
                    ada_product(OUT_AT[i + 1], 1)
            if u < N_OUT - 1:
                split_lo(U_OUT + 2 + u)

        def mlp(l, ch, first=False, last=False):
            if first:
                for tb in range(NTB):
                    apply_xn(2 * l + 1, tb)
            if first:
                pool.wait_ge(h_lo, GRP * (l + 2))
            split_lo(U_MLP[l] + 2 * ch + 1, (U_MLP[l] + 1) % 2)
            if l == 0:
                ada_product(ADA_L0 + ADA_BATCH * ch, 1)
                ada_product(ADA_L0 + ADA_BATCH * ch + 1, 1)
            if not (l == 1 and last):
                split_lo(U_MLP[l] + 2 * ch + 2, U_MLP[l] % 2)
            if l == 0:
                ada_product(ADA_L0 + ADA_BATCH * ch + 2, 1)
            if last:
                for i in range(GRP):
                    add_square(2 * l + 2, i)

        mlp(0, 0, first=True)
        with pool.Fori(1, NCH - 1) as ch:
            mlp(0, ch)
        mlp(0, NCH - 1, last=True)

        segs = ((PADW, 0, SAMPLE), (SAMPLE + 3 * PADW, SAMPLE, PROMPT))
        pool.wait_ge(m2_mm[0], GRP * NCH)
        for i in range(2):
            for p0, w in ((0, PADW), (PADW + SAMPLE, 2 * PADW), (PW - PADW, PADW)):
                z = nc.gpsimd.memset(prow[i][0][:, p0:p0 + w], 0.0)
        z.then_inc(pz_ok, 1)
        pool.wait_ge(rstd_ok, NTB * 3)

        def pool_xn(n):
            d = POOL_TILES[n]
            after(pool, pp, n - 1)
            for p0, t0, w in segs:
                e = nc.gpsimd.tensor_tensor(prow[n % 2][0][:, p0:p0 + w], X[:, d, t0:t0 + w], acc2[0][:, t0:t0 + w], ALU.mult)
            e.then_inc(pxn, 1)

        def pool_lo(n):
            d = POOL_TILES[n]
            pool.wait_ge(p_hi, n + 1)
            for p0, t0, w in segs:
                e = nc.gpsimd.tensor_tensor(hL[:, d, t0:t0 + w], prow[n % 2][pool_dst(d)][:, p0:p0 + w],
                                            hH[:, d, t0:t0 + w].bitcast(F32), ALU.subtract)
            e.then_inc(p_lo, 1)

        pool_xn(0)
        pool_xn(1)
        split_lo(U_MLP[1])
        for n in range(DT):
            if n + 2 < DT:
                pool_xn(n + 2)
            pool_lo(n)

        mlp(1, 0, first=True)
        with pool.Fori(1, NCH - 1) as ch:
            mlp(1, ch)
        mlp(1, NCH - 1, last=True)

    @block.vector
    def _(dve):
        V = nc.vector

        def rstd(q, tb):
            dve.wait_ge(rms_ok, NTB * q + tb + 1)
            V.reciprocal(acc2[q % 2][:, cols(tb)], acc2[q % 2][:, cols(tb)]).then_inc(rstd_ok, 1)

        def gains(q):
            l, m = q // 2, q % 2
            v0 = (32 if m else 16) + DT * l
            V.scalar_tensor_tensor(out=gain[q][:, :, :], in0=mod[:, l, 3 * DT * m + DT:3 * DT * m + 2 * DT, :], scalar=1.0,
                                   in1=vec[:, v0:v0 + DT].unsqueeze(2).to_broadcast([P, DT, 2]),
                                   op0=ALU.add, op1=ALU.mult).then_inc(gain_ok, 1)

        def mods(l, j0, j1, col, nth, copies=2):
            V.tensor_tensor(mod[:, l, j0:j1, :],
                            ADA_BANK[:, col:col + 2 * copies * (j1 - j0)].rearrange("p (j c r) -> p j c r", c=2, r=copies)[:, :, :, 0],
                            adab[:, NMOD * l + j0:NMOD * l + j1].unsqueeze(2).to_broadcast([P, j1 - j0, 2]),
                            ALU.add).then_inc(mod_ok, 1)
            dve.wait_ge(mod_ok, nth)

        def apply(q, tb):
            w, cond = TB[tb][1:]

            def modulated(d):
                i = GRP * TURN[q] + DT * tb + d
                if q == 0:
                    dve.wait_ge(*xn_done(tb, d))
                    src = xnT[:, d, cols(tb)]
                else:
                    dve.wait_ge(xn_ok, xn_total(q) + DT * tb + d + 1)
                    src = xn_b[i % 2][:, 0:w]
                after(dve, h_lo, i - 1)
                V.tensor_scalar(hs_b[i % 2][:, 0:w], src, gain[q][:, d, cond:cond + 1], shift(q, d, cond),
                                ALU.mult, ALU.add).then_inc(hs_ok, 1)

            def lower(d):
                i = GRP * TURN[q] + DT * tb + d
                dve.wait_ge(h_hi, i + 1)
                dve.wait_ge(hs_ok, i + 1)
                V.tensor_tensor(hL[:, d, cols(tb)], hs_b[i % 2][:, 0:w], hH[:, d, cols(tb)].bitcast(F32),
                                ALU.subtract).then_inc(h_lo, 1)

            for d in range(DT):
                if q > 0 and tb == 0 and d in (3, 6):
                    rstd(q, d // 3)
                if q > 0 and d > 0:
                    lower(d - 1)
                modulated(d)
                if q == 0 and d > 0:
                    lower(d - 1)
            lower(DT - 1)

        def ada_reduce(n, j, pr, batch):
            if pr == 1 and j == 0:
                after(dve, a_mm, batch)
            elif j == 0:
                after(dve, a_slo, batch)
            for i, src in enumerate((ada_pr[pr], ada_st)):
                dve.wait_ge(a_pr, 2 * n + i + 1)
                e = V.tensor_reduce(ada_sum[pr][:, j, i, :], src[:, :, :].rearrange("p k n -> p n k"), mybir.AxisListType.X,
                                    ALU.add)
            e.then_inc(a_sum, 1)

        def ada_halves(n, pr, batch, tiles=ADA_BATCH):
            dve.wait_ge(a_sum, n + 1)
            after(dve, a_mm, batch)
            V.tensor_copy(ada_sH[pr][:, 0:tiles, :, :], ada_sum[pr][:, 0:tiles, :, :]).then_inc(a_shi, 1)
            dve.wait_ge(a_shi, batch + 1)
            V.tensor_tensor(ada_sL[pr][:, 0:tiles, :, :], ada_sum[pr][:, 0:tiles, :, :], ada_sH[pr][:, 0:tiles, :, :].bitcast(F32),
                            ALU.subtract).then_inc(a_slo, 1)

        def update(mm, n, ev, src, gate_ap, t, d, own=None):
            dve.wait_ge(mm, n)
            if own is not None:
                after(dve, *own)
            V.scalar_tensor_tensor(out=X[:, d, cols(t)], in0=src[:, 0:TB[t][1]], scalar=gate_ap, in1=X[:, d, cols(t)],
                                   op0=ALU.mult, op1=ALU.add).then_inc(ev, 1)

        dve.wait_ge(fill_ok, 2)
        V.tensor_copy(ones_r[:, :], ones[:, 0:8]).then_inc(ones_ok, 1)
        dve.wait_ge(dec_exp, 1)
        V.tensor_scalar(ned[:, :], dec[:, :], -1.0, None, ALU.mult).then_inc(dec_neg, 1)
        dve.wait_ge(vec_mm, 1)
        V.tensor_copy(vec[:, :], bank[5][:, 0:68]).then_inc(vec_ev, 1)
        dve.wait_ge(vec_mm, 2)
        V.tensor_copy(adab[:, :], bank[4][:, 0:2 * NMOD]).then_inc(vec_ev, 1)
        for i, (t, d) in enumerate(BY_BLOCK):
            dve.wait_ge(xt_mm, i + 1)
            V.tensor_copy(X[:, d, cols(t)], bank[i % 4][:, 0:TB[t][1]]).then_inc(xt_ev, 1)
        for tb in range(NTB):
            rstd(0, tb)
            dve.wait_ge(rstd_ok, tb + 1)
            for d in range(1, DT, 2):
                V.tensor_tensor(xnT[:, d, cols(tb)], X[:, d, cols(tb)], acc2[0][:, cols(tb)], ALU.mult).then_inc(xn_v, 1)
        dve.wait_ge(row_mm, 1)
        dve.wait_ge(vec_ev, 2)
        mods(0, 0, 2 * DT, 0, 1, 1)
        gains(0)
        dve.wait_ge(gain_ok, 1)
        for tb in range(NTB):
            apply(0, tb)
        def ada_batch(b):
            for j in range(ADA_BATCH):
                ada_reduce(ADA_BATCH * b + j, j, 0, b)
            ada_halves(ADA_BATCH * b + ADA_BATCH - 1, 0, b)

        ada_batch(0)
        for n in range(NT):
            dve.wait_ge(in_ev, IN_CUM[1] + n + 1)
            for g in range(4):
                e = V.bn_stats(vst[:, 4 * n + g, :], vtok[:, n, g * P:(g + 1) * P])
            e.then_inc(v_bn, 1)
            dve.wait_ge(v_bn, n + 1)
            for g in range(4):
                e = V.bn_aggr(vmv[:, 4 * n + g, :], vst[:, 4 * n + g, :])
            e.then_inc(v_stat, 1)
        dve.wait_ge(v_sd, 1)
        V.reciprocal(vmv[:, :, 1], vmv[:, :, 1]).then_inc(v_rstd, 1)
        dve.wait_ge(v_rstd, 1)
        for n in range(NT):
            for g in range(4):
                a, j = vtok[:, n, g * P:(g + 1) * P], 4 * n + g
                e = V.tensor_scalar(a, a, vmv[:, j, 0:1], vmv[:, j, 1:2], ALU.subtract, ALU.mult)
            e.then_inc(v_norm, 1)
        dve.wait_ge(ws_mm, 1)
        V.tensor_copy(wsT[:, :, :].rearrange("p g i -> p (g i)"), WS_BANK[:, :]).then_inc(ws_ev, 1)
        dve.wait_ge(ws_in, 32)
        for half in range(HT):
            ui = 3 + half
            b = ADA_IN_UNITS[ui]
            for g6 in range(NTB * HT):
                i, tb = NTB * HT * half + g6, g6 // HT
                g, w = HT * half + g6 % HT, TB[tb][1]
                dve.wait_ge(sp_mm, i + 1)
                after(dve, a_lo, i - 1)
                chunks = dict(c=w // P)
                V.scalar_tensor_tensor(out=ga[i % 2][:, 0:w].rearrange("p (c i) -> p c i", **chunks),
                                       in0=bank[4 + i % 2][:, 0:w].rearrange("p (c i) -> p c i", **chunks),
                                       scalar=vec[:, 64 + g:65 + g],
                                       in1=bias_b[:, g, :].unsqueeze(1).to_broadcast([P, w // P, P]),
                                       op0=ALU.mult, op1=ALU.add).then_inc(t_ok, 1)
                dve.wait_ge(t_ok, i + 1)
                dve.wait_ge(in_ev, IN_CUM[ui] + g6 + 1)
                V.tensor_tensor(ga[i % 2][:, 0:w], ga[i % 2][:, 0:w], ug[i % 2][:, 0:w], ALU.mult).then_inc(a_ok, 1)
                if g6 % 2 == 1:
                    ada_reduce(ADA_BATCH * b + g6 // 2, g6 // 2, 0, b)
            ada_halves(ADA_BATCH * b + ADA_BATCH - 1, 0, b)
        dve.wait_ge(rope_in, 16)
        for hd in range(2 * HEADS):
            dve.wait_ge(swap_in[hd % 2], 32 * (hd // 2 + 1))
            V.tensor_tensor(swap[hd % 2][:, :], swap[hd % 2][:, :], rope[:, 1, :], ALU.mult).then_inc(rot_s, 1)
            dve.wait_ge(rot_s, hd + 1)
            dve.wait_ge(rot_c, hd + 1)
            V.tensor_tensor(qk[:, hd, 0:SAMPLE], qk[:, hd, 0:SAMPLE], swap[hd % 2][:, :], ALU.add).then_inc(rot_ok, 1)
            if hd % 2 == 1:
                ada_batch(3 + hd // 2)
        ada_batch(BATCHES_IN - 1)
        dve.wait_ge(a_mm, BATCHES_IN)
        mods(0, 2 * DT, 5 * DT, ADA_COL0, 2)
        gains(1)

        dve.wait_ge(dec_tab, 3)
        dve.wait_ge(state_in, 32)
        for j, st in enumerate(ADVANCE):
            for d in range(2):
                dve.wait_ge(kt_mm, 2 * j + d + 1)
                after(dve, kv_mm, 2 * (j - 2) + d + 1)
                V.tensor_tensor(kx[j % 2][:, d, :, :], bank[4 + d][:, :].rearrange("p (h e) -> p h e", h=HEADS),
                                kd[:, 4 * d:4 * d + 4].unsqueeze(2).to_broadcast([P, HEADS, P]), ALU.mult).then_inc(kx_ok, 1)
            for d in range(2):
                src, dst = S[d][st % 2], S[d][(st + 1) % 2]
                dve.wait_ge(kv_mm, 2 * j + d + 1)
                after(dve, s_ok, 2 * (j - 1) + d + 1)
                if st == NS:
                    dve.wait_ge(zero_ok, 2)
                after(dve, s_out[(st + 1) % 2], 16 * 2 * ((st + 1) // 2))
                for h in range(HEADS):
                    e = V.scalar_tensor_tensor(out=dst[:, h, :], in0=src[:, h, :], scalar=cd[:, 4 * d + h:4 * d + h + 1],
                                               in1=bank[6 + d][:, h * P:(h + 1) * P], op0=ALU.mult, op1=ALU.add)
                e.then_inc(s_ok, 1)
        dve.wait_ge(tab_ok, 2)
        dve.wait_ge(gate_out, 32 * 4)
        for k in range(NT + 3):
            if k < NT:
                dve.wait_ge(sc_mm, k + 1)
                after(dve, y_mm, 2 * (k - 1))
                for d in range(2):
                    V.tensor_tensor(pt[k % 2][:, d, :, :], bank[k % 2][:, :].rearrange("p (h i) -> p h i", h=HEADS),
                                    tab[:, d, :, :], ALU.mult).then_inc(pt_ok, 1)
            m = k - 2
            if 0 <= m < NT:
                dve.wait_ge(yn_ok, 2 * m + 1)
                dve.wait_ge(gate_in[m % 2], 32 * (m // 2 + 1))
                y0 = yn[m % 2][:, 0, :, :].rearrange("p h e -> p (h e)")
                V.tensor_tensor(y0, y0, gt[m % 2][:, 0, :, :].rearrange("p a n -> p (a n)"), ALU.mult).then_inc(gm_f, 1)
            n = k - 1
            if 0 <= n < NT:
                for d in range(2):
                    dve.wait_ge(y_mm, 2 * n + d + 1)
                    for h in range(HEADS):
                        e = V.bn_stats(rst[n % 2][:, HEADS * d + h, :], bank[2 + 2 * (n % 2) + d][:, h * P:(h + 1) * P])
                e.then_inc(y_bn, 1)
                dve.wait_ge(y_bn, n + 1)
                after(dve, yn_ok, 2 * (n - 1))
                for j in range(2 * HEADS):
                    e = V.bn_aggr(rmv[n % 2][:, j, :], rst[n % 2][:, j, :])
                e.then_inc(y_stat, 1)
            m = k - 3
            if 0 <= m < NT:
                dve.wait_ge(b_hi, m + 1)
                V.tensor_tensor(hL[:, HEADS:DT, m * P:(m + 1) * P], bank[6 + m % 2][:, :].rearrange("p (h i) -> p h i", h=HEADS),
                                hH[:, HEADS:DT, m * P:(m + 1) * P].bitcast(F32), ALU.subtract).then_inc(b_lo, 1)
            if 0 <= n < NT:
                dve.wait_ge(y_sd, n + 1)
                V.reciprocal(rmv[n % 2][:, :, 1], rmv[n % 2][:, :, 1]).then_inc(y_rstd, 1)
                dve.wait_ge(y_rstd, n + 1)
                V.scalar_tensor_tensor(out=rnm[n % 2][:, :], in0=rmv[n % 2][:, :, 0], scalar=-1.0, in1=rmv[n % 2][:, :, 1],
                                       op0=ALU.mult, op1=ALU.mult).then_inc(y_nmr, 1)

        dve.wait_ge(mod_ok, 2)
        for i, (t, d) in enumerate(BY_PAIR):
            if d == 0:
                dve.wait_ge(x_back[t], 32 if t == 0 else 16)
            update(out_mm, i + 1, out_ev, bank[i % 4], mod[:, 0, 2 * DT + d, TB[t][2]:TB[t][2] + 1], t, d)
            if i == GRP - NTB:
                rstd(1, 0)
            if i in OUT_AT:
                b, j = divmod(OUT_AT[i] - ADA_IN, ADA_BATCH)
                ada_reduce(OUT_AT[i], j, 1, BATCHES_IN + b)
                if OUT_AT[i] == ADA_OUT_TILES[b][-1]:
                    ada_halves(OUT_AT[i], 1, BATCHES_IN + b, j + 1)
        dve.wait_ge(a_mm, BATCHES_L0)
        mods(0, 5 * DT, NMOD, ADA_COL0 + 4 * 3 * DT, 3)

        def mlp(l, ch, first=False, last=False):
            n0 = NTB * HT * ch
            n_ada = ADA_L0 + ADA_BATCH * ch

            def hidden_lo(g):
                dve.wait_ge(mid_hi[l], n0 + g + 1)
                w = TB[g // HT][1]
                V.tensor_tensor(midL[:, g % HT, cols(g // HT)], r_b[g % 3][:, 0:w],
                                midH[:, g % HT, cols(g // HT)].bitcast(F32), ALU.subtract).then_inc(mid_lo[l], 1)

            if first:
                dve.wait_ge(gain_ok, 2 if l == 0 else 5)
                for tb in range(NTB):
                    apply(2 * l + 1, tb)
            for g in range(NTB * HT):
                dve.wait_ge(relu_ok[l], n0 + g + 1)
                r = r_b[g % 3][:, 0:TB[g // HT][1]]
                V.tensor_tensor(r, r, r, ALU.mult).then_inc(sqr_ok[l], 1)
                if g > 0:
                    hidden_lo(g - 1)
                if l == 0 and g == 1:
                    ada_reduce(n_ada, 0, 1, BATCHES_L0 + ch)
            hidden_lo(NTB * HT - 1)
            for i, (t, d) in enumerate(BY_BLOCK):
                if l == 0 and i in (1, DT + 1):
                    j = 1 + i // DT
                    ada_reduce(n_ada + j, j, 1, BATCHES_L0 + ch)
                if l == 0 and i == DT + 4:
                    ada_halves(n_ada + ADA_BATCH - 1, 1, BATCHES_L0 + ch)
                n = GRP * ch + i
                update(m2_mm[l], n + 1, m2_ev[l], bank[2 + i % 4], mod[:, l, 5 * DT + d, TB[t][2]:TB[t][2] + 1], t, d,
                       (m2_ev[l], n + 1 - GRP))
            if last and l == 0:
                for tb in range(NTB):
                    rstd(2, tb)

        mlp(0, 0, first=True)
        with dve.Fori(1, NCH - 1) as ch:
            mlp(0, ch)
        mlp(0, NCH - 1, last=True)

        dve.wait_ge(a_mm, BATCHES_L0 + NCH)
        mods(1, 0, NMOD, 0, 4)
        gains(2)
        V.tensor_tensor(gpool[:, :, :], mod[:, 1, 2 * DT:3 * DT, :], vec[:, 56:56 + DT].unsqueeze(2).to_broadcast([P, DT, 2]),
                        ALU.mult).then_inc(gain_ok, 1)
        gains(3)
        dve.wait_ge(gain_ok, 5)

        def pooled(n):
            d = POOL_TILES[n]
            g = d // 2
            row = prow[n % 2]
            dve.wait_ge(ph, n + 1)
            after(dve, p_lo, n - 1)
            steps = [(1, 0, (1, PW), 1, 0), (2, 1, (2, PW - 1), 1, 1), (1, 2, (4, PW - 3), 2, 2), (2, 1, (8, PW - 7), 4, 4)]
            for dst, src, (a, b), back, ahead in steps[:g + 1]:
                V.tensor_tensor(row[dst][:, a:b], row[src][:, a - back:b - back], row[src][:, a + ahead:b + ahead],
                                ALU.add).then_inc(pw, 1)
                pw_n[0] += 1
                dve.wait_ge(pw, pw_n[0])
            res = row[pool_dst(d)]
            for p0, w in ((PADW, SAMPLE), (SAMPLE + 3 * PADW, PROMPT)):
                for side, a in ((0, p0), (1, p0 + w - PADW)):
                    e = V.tensor_tensor(res[:, a:a + PADW], res[:, a:a + PADW], edges[:, g, side, :], ALU.mult)
            e.then_inc(pe_ok, 1)
            dve.wait_ge(pe_ok, n + 1)
            V.scalar_tensor_tensor(out=res[:, PADW:PW - PADW], in0=res[:, PADW:PW - PADW], scalar=1.0 / WINDOWS[g],
                                   in1=row[0][:, PADW:PW - PADW], op0=ALU.mult, op1=ALU.subtract).then_inc(pp, 1)

        def pool_updates(n):
            for i in range(PAIRS * n, PAIRS * (n + 1)):
                if i == GRP - NTB + 1:
                    rstd(3, 0)
                t, d = BY_POOL[i]
                update(pool_mm, i + 1, pool_ev, bank[i % 4], gpool[:, d, TB[t][2]:TB[t][2] + 1], t, d)

        pw_n = [0]
        dve.wait_ge(pz_ok, 1)
        for n in range(DT):
            pooled(n)
            if n >= 3 and n % 2 == 1:
                pool_updates(n // 2 - 1)
        pool_updates(DT // 2 - 1)

        mlp(1, 0, first=True)
        with dve.Fori(1, NCH - 1) as ch:
            mlp(1, ch)
        mlp(1, NCH - 1, last=True)

        for t, d in BY_BLOCK:
            if d == 0:
                rstd(4, t)
                dve.wait_ge(rstd_ok, NTB * 4 + t + 1)
            V.scalar_tensor_tensor(out=yT[:, d, cols(t)], in0=X[:, d, cols(t)], scalar=vec[:, 48 + d:49 + d],
                                   in1=acc2[0][:, cols(t)], op0=ALU.mult, op1=ALU.mult).then_inc(yt_ok, 1)
        for n in range(NT):
            dve.wait_ge(yt_mm, 2 * n + 2)
            V.tensor_copy(ytok[:, n, 512:1024], bank[(2 * n + 1) % 4][:, :]).then_inc(yt_evv, 1)

    @block.tensor
    def _(pe):
        def ada_total(batch, tiles, pr, col):
            pe.wait_ge(a_slo, batch + 1)
            for j in range(tiles):
                for i in range(2):
                    out = ADA_BANK[:, col(4 * j + 2 * i)]
                    nc.tensor.matmul(out, ada_sH[pr][:, j, i, :], ones_r[:, 0:2], start=True, stop=False)
                    mm = nc.tensor.matmul(out, ada_sL[pr][:, j, i, :], ones_r[:, 0:2], start=False, stop=True)
            mm.then_inc(a_mm, 1)

        def total(q, tb):
            need = 1 + max(a for (t, d), a in ADDS[q].items() if t == tb and a is not None)
            pe.wait_ge(sum_add, ADD_BASE[q] + need)
            nc.tensor.matmul(total_bank(q, tb)[:, 0:TB[tb][1]], ones[:, :], acc2[q % 2][:, cols(tb)], start=True,
                             stop=True).then_inc(sum_mm, 1)

        pe.wait_ge(const_in, 16 * 10)
        nc.tensor.transpose(bank[5][:, 0:68], rows[0:68, :], ident[0:68, 0:68]).then_inc(vec_mm, 1)
        nc.tensor.transpose(bank[4][:, 0:2 * NMOD], ada_rows[0:2 * NMOD, :], ident[0:2 * NMOD, 0:2 * NMOD]).then_inc(vec_mm, 1)
        pe.wait_ge(fill_ok, 2)
        for tb in range(NTB):
            pe.wait_ge(x_loaded[tb], 16)
            n0 = TB[tb][0] // P
            for d in range(DT):
                i = DT * tb + d
                after(pe, xt_ev, i - 3)
                for n in range(TB[tb][1] // P):
                    mm = nc.tensor.transpose(bank[i % 4][:, n * P:(n + 1) * P], xtok[:, n0 + n, d * P:(d + 1) * P], ident)
                mm.then_inc(xt_mm, 1)
        pe.wait_ge(silu_ok, 1)
        pe.wait_ge(xt_ev, GRP)
        for i in range(8):
            pe.wait_ge(ada0_in[i], 16)
            for k in range(DT):
                mm = nc.tensor.matmul(bank[i // 2][0:2, UC * (i % 2):UC * (i % 2 + 1)], sc2[:, k, :], ada0[i][:, k, :],
                                      start=(k == 0), stop=(k == DT - 1))
            mm.then_inc(ada0_mm, 1)
            if i in (0, 3, 5):
                total(0, (0, 3, 5).index(i))
        for j in range(2 * DT):
            after(pe, row_ok, j // 4 + 1)
            mm = nc.tensor.transpose(ADA_BANK[:, 2 * j:2 * j + 2], mod_rows[0:2, j * P:(j + 1) * P], ident[0:2, 0:2])
        mm.then_inc(row_mm, 1)

        def state_keys(st):
            j = ADVANCE.index(st)
            for d in range(2):
                n = RSTEPS[st][d]
                if j == 0:
                    pe.wait_ge(rot_ok, 2 * HEADS)
                after(pe, kx_ok, 2 * (j - 1) + d + 1)
                for h in range(HEADS):
                    mm = nc.tensor.transpose(bank[4 + d][:, h * P:(h + 1) * P], qk[:, HEADS + h, n * P:(n + 1) * P], ident)
                mm.then_inc(kt_mm, 1)

        def state_values(st):
            j = ADVANCE.index(st)
            for d in range(2):
                n = RSTEPS[st][d]
                pe.wait_ge(kx_ok, 2 * j + d + 1)
                after(pe, s_ok, 2 * (j - 1) + d + 1)
                if j == 0:
                    pe.wait_ge(mod_ok, 2)
                for h in range(HEADS):
                    mm = nc.tensor.matmul(bank[6 + d][:, h * P:(h + 1) * P], kx[j % 2][:, d, h, :],
                                          val[:, n, h * P:(h + 1) * P], start=True, stop=True)
                mm.then_inc(kv_mm, 1)

        G = 0
        pe.wait_ge(mod_ok, 1)
        for ui, (kind, half, _, tok) in enumerate(IN_UNITS):
            pe.wait_ge(w_lo, ui + 1)
            wH, wL = (r[ui % 2][:, :].rearrange("p (k n) -> p k n", k=DT) for r in (ringH, ringL))
            if ui == 0:
                for tb in range(NTB):
                    for k in range(DT):
                        pe.wait_ge(h_lo, DT * tb + k + 1)
                        for g in range(TB[tb][0] // P, (TB[tb][0] + TB[tb][1]) // P):
                            if k == 0:
                                after(pe, in_ev, g - 7)
                            ts = slice(g * P, (g + 1) * P)
                            mm = pair_pass(bank[g % 8][:, 0:UC], wH[:, k, :], wL[:, k, :], hH[:, k, ts], hL[:, k, ts],
                                           k == 0, k == DT - 1, weights_moving=True)
                            if k == DT - 1:
                                mm.then_inc(in_mm, 1)
                G = IN_GROUPS[0]
            for g in range(IN_GROUPS[ui] if ui > 0 else 0):
                tb = (0 if g < 4 else 1 if g < 8 else 2) if tok else g // HT
                after(pe, in_ev, G - 3)
                for k in range(DT):
                    if tok:
                        ts = slice(g * P, (g + 1) * P)
                        mm = pair_pass(bank[G % 4][:, 0:UC], wH[:, k, :], wL[:, k, :], hH[:, k, ts], hL[:, k, ts],
                                       k == 0, k == DT - 1, weights_moving=True)
                    else:
                        fs = slice((g % HT) * P, (g % HT + 1) * P)
                        mm = pair_pass(bank[G % 4][:, 0:TB[tb][1]], wH[:, k, fs], wL[:, k, fs], hH[:, k, cols(tb)],
                                       hL[:, k, cols(tb)], k == 0, k == DT - 1)
                mm.then_inc(in_mm, 1)
                G += 1
                if kind == "u":
                    i = NTB * HT * half + g
                    if i == 0:
                        pe.wait_ge(v_norm, NT)
                        pe.wait_ge(ws_ev, 1)
                    after(pe, t_ok, i - 1)
                    for n in range(TB[tb][1] // P):
                        ch = TB[tb][0] // P + n
                        gg = HT * half + g % HT
                        mm = nc.tensor.matmul(bank[4 + i % 2][:, n * P:(n + 1) * P], vtok[:, ch, gg * P:(gg + 1) * P],
                                              wsT[:, gg, :], start=True, stop=True)
                    mm.then_inc(sp_mm, 1)
                if ui in R_UNITS and g % 2 == 1 and g // 2 < len(R_UNITS[ui]) and R_UNITS[ui][g // 2] in ADVANCE:
                    state_keys(R_UNITS[ui][g // 2])
                if ui in R_UNITS and g % 2 == 0 and g > 0 and g // 2 - 1 < len(R_UNITS[ui]) and R_UNITS[ui][g // 2 - 1] in ADVANCE:
                    state_values(R_UNITS[ui][g // 2 - 1])
            if ui - 1 in ADA_IN_UNITS:
                b = ADA_IN_UNITS[ui - 1]
                c0 = ADA_COL0 + 4 * ADA_BATCH * b
                ada_total(b, ADA_BATCH, 0, lambda i: slice(c0 + i, c0 + i + 2))
            if ui == 1:
                pe.wait_ge(ws_in, 32)
                for g in range(4):
                    mm = nc.tensor.transpose(WS_BANK[:, g * P:(g + 1) * P], ws_raw[:, g, :], ident)
                mm.then_inc(ws_mm, 1)

        def out_product(G):
            u, g = divmod(G, NTB * HT)
            U = U_OUT + u
            wH, wL = (r[U % 2][:, :].rearrange("p (k n) -> p k n", k=DT) for r in (ringH, ringL))
            tb, fs = g // HT, slice((g % HT) * P, (g % HT + 1) * P)
            if g == 0:
                pe.wait_ge(w_lo, U + 1)
            if u == 0:
                pe.wait_ge(b_lo, min(4 * (tb + 1), NT))
            after(pe, out_ev, G - 3)
            order = [4, 5, 6, 7, 0, 1, 2, 3]
            for k in order:
                if G == 0 and k == 0:
                    pe.wait_ge(a_back, 16 * 2 * HEADS)
                mm = pair_pass(bank[G % 4][:, 0:TB[tb][1]], wH[:, k, fs], wL[:, k, fs], hH[:, k, cols(tb)],
                               hL[:, k, cols(tb)], k == order[0], k == order[-1])
            mm.then_inc(out_mm, 1)

        pe.wait_ge(in_ev, G)
        pe.wait_ge(s_ok, 2 * len(ADVANCE))
        for k in range(NT + 3):
            if k < NT:
                after(pe, pt_ok, 2 * (k - 1))
                for h in range(HEADS):
                    mm = nc.tensor.matmul(bank[k % 2][:, h * P:(h + 1) * P], qk[:, HEADS + h, k * P:(k + 1) * P],
                                          qk[:, h, k * P:(k + 1) * P], start=True, stop=True)
                mm.then_inc(sc_mm, 1)
            m = k - 3
            if m == NT - 1:
                out_product(0)
            if 0 <= m < NT:
                pe.wait_ge(b_ok, m + 1)
                after(pe, b_lo, m - 1)
                for h in range(HEADS):
                    mm = nc.tensor.transpose(bank[6 + m % 2][:, h * P:(h + 1) * P], yn[m % 2][:, 0, h, :], ident)
                mm.then_inc(bt_mm, 1)
            n = k - 1
            if 0 <= n < NT:
                pe.wait_ge(s_back[n % 2], 32 * (n // 2 + 1))
                for d in range(2):
                    pe.wait_ge(pt_ok, 2 * n + d + 1)
                    pe.wait_ge(qd_ok, 2 * n + d + 1)
                    after(pe, yn_ok, 2 * (n - 2) + d + 1)
                    for h in range(HEADS):
                        out = bank[2 + 2 * (n % 2) + d][:, h * P:(h + 1) * P]
                        nc.tensor.matmul(out, pt[n % 2][:, d, h, :], val[:, n, h * P:(h + 1) * P], start=True, stop=False)
                        mm = nc.tensor.matmul(out, qd[n % 2][:, d, h, :], S[d][n % 2][:, h, :], start=False, stop=True)
                    mm.then_inc(y_mm, 1)

        for G in range(1, N_OUT * NTB * HT):
            out_product(G)
            if G in OUT_TOTAL_AT:
                b = OUT_TOTAL_AT[G]
                c1 = ADA_COL0 + 4 * ADA_OUT_TILES[b][0]
                ada_total(BATCHES_IN + b, len(ADA_OUT_TILES[b]), 1, lambda i: slice(c1 + i, c1 + i + 2))
            if G == GRP - NTB:
                total(1, 0)

        def ada_of_chunk(ch):
            c2 = 4 * ADA_BATCH * ch
            ada_total(BATCHES_L0 + ch, ADA_BATCH, 1,
                      lambda i: slice(c2 + i, c2 + i + 2) if isinstance(ch, int) else bass.ds(c2 + i, 2))

        def mlp(l, ch, first=False, last=False):
            UA, n0 = U_MLP[l] + 2 * ch, NTB * HT * ch
            sa, sb_ = U_MLP[l] % 2, (U_MLP[l] + 1) % 2
            aH, aL = (r[sa][:, :].rearrange("p (k n) -> p k n", k=DT) for r in (ringH, ringL))
            bH, bL = (r[sb_][:, :].rearrange("p (k n) -> p k n", k=HT) for r in (ringH, ringL))
            pe.wait_ge(w_lo, UA + 1)
            if first:
                for tb in range(2):
                    for k in range(DT):
                        if l == 0 and tb == 0 and k in (1, 3):
                            total(1, 1 + k // 3)
                        pe.wait_ge(h_lo, GRP * (l + 1) + DT * tb + k + 1)
                        for f in range(HT):
                            mm = pair_pass(bank[HT * tb + f][:, 0:TB[tb][1]], aH[:, k, f * P:(f + 1) * P],
                                           aL[:, k, f * P:(f + 1) * P], hH[:, k, cols(tb)], hL[:, k, cols(tb)],
                                           k == 0, k == DT - 1)
                            if k == DT - 1:
                                mm.then_inc(m1_mm[l], 1)
            for tb in range(2 if first else 0, NTB):
                if first:
                    pe.wait_ge(h_lo, GRP * (l + 1) + DT * (tb + 1))
                for f in range(HT):
                    g = HT * tb + f
                    after(pe, relu_ok[l], g - 3 if first else n0 + g - 1)
                    for k in range(DT):
                        mm = pair_pass(bank[g % 2][:, 0:TB[tb][1]], aH[:, k, f * P:(f + 1) * P], aL[:, k, f * P:(f + 1) * P],
                                       hH[:, k, cols(tb)], hL[:, k, cols(tb)], k == 0, k == DT - 1)
                    mm.then_inc(m1_mm[l], 1)
                if tb == 0 and l == 0 and not first:
                    ada_of_chunk(ch - 1)
            pe.wait_ge(w_lo, UA + 2)
            if first:
                pe.wait_ge(relu_ok[l], 2 * HT)
            for tb in range(NTB):
                pe.wait_ge(mid_lo[l], n0 + HT * (tb + 1))
                for d in range(DT):
                    i = DT * tb + d
                    after(pe, m2_ev[l], GRP * ch + i - 3)
                    for k in range(HT):
                        mm = pair_pass(bank[2 + i % 4][:, 0:TB[tb][1]], bH[:, k, d * P:(d + 1) * P], bL[:, k, d * P:(d + 1) * P],
                                       midH[:, k, cols(tb)], midL[:, k, cols(tb)], k == 0, k == HT - 1)
                    mm.then_inc(m2_mm[l], 1)
                if last and tb > 0:
                    total(2 * l + 2, tb - 1)
            if last:
                total(2 * l + 2, NTB - 1)

        mlp(0, 0, first=True)
        with pe.Fori(1, NCH - 1) as ch:
            mlp(0, ch)
        mlp(0, NCH - 1, last=True)
        ada_of_chunk(NCH - 1)

        pe.wait_ge(w_lo, U_POOL + 1)
        wH, wL = (r[U_POOL % 2][:, :].rearrange("p (k n) -> p k n", k=DT) for r in (ringH, ringL))
        def add_square(i):
            t, d = BY_POOL[i]
            pe.wait_ge(sq_ok, GRP * 3 + i + 1)
            nc.tensor.matmul(total_bank(3, t)[:, 0:TB[t][1]], ones[:, :], sq_b[i % 2][:, 0:TB[t][1]], start=d == POOL_TILES[0],
                             stop=d == POOL_TILES[-1]).then_inc(sq_mm, 1)

        for i, (tb, d) in enumerate(BY_POOL):
            g, n = d // 2, i // PAIRS
            if i > 0 and i % PAIRS == 0:
                for j in range(PAIRS * (n - 1), PAIRS * n):
                    add_square(j)
            pe.wait_ge(p_lo, 2 * n + 2)
            after(pe, pool_ev, i - 3)
            fs = slice((d % 2) * P, (d % 2 + 1) * P)
            for k in (2 * g, 2 * g + 1):
                mm = pair_pass(bank[i % 4][:, 0:TB[tb][1]], wH[:, k, fs], wL[:, k, fs], hH[:, k, cols(tb)], hL[:, k, cols(tb)],
                               k == 2 * g, k == 2 * g + 1)
            mm.then_inc(pool_mm, 1)
        for j in range(GRP - PAIRS, GRP):
            add_square(j)

        mlp(1, 0, first=True)
        with pe.Fori(1, NCH - 1) as ch:
            mlp(1, ch)
        mlp(1, NCH - 1, last=True)
        pe.wait_ge(rms_ok, NTB * 5)
        for n in range(NT):
            tb = 0 if n < 4 else 1 if n < 8 else 2
            pe.wait_ge(yt_ok, DT * (tb + 1))
            for half, ev in ((0, yt_eva), (1, yt_evv)):
                after(pe, ev, n - 1)
                for j in range(4):
                    mm = nc.tensor.transpose(bank[(2 * n + half) % 4][:, j * P:(j + 1) * P], yT[:, 4 * half + j, n * P:(n + 1) * P],
                                             ident)
                mm.then_inc(yt_mm, 1)


_INS = ["x_prompt", "x_sample", "state_ret", "c", "c_ctx", "ada_w", "ada_b", "norm_mix", "norm_mlp", "mlp_w1", "mlp_w2",
        "ev_w_in", "ev_w_s", "ev_b_s", "ev_vnorm", "ev_decay", "ev_w_out", "od_w_pool", "od_pool_scale", "final_norm"]
_OUTS = [((1, PROMPT, D), "float32"), ((1, SAMPLE, D), "float32"), ((1, 1, 2, HEADS, P, P), "float32")]


def constants():
    j = np.arange(P, dtype=np.float32)
    small = np.ones((P, P + 2 + 64), np.float32)
    small[:, 0:P] = np.eye(P, dtype=np.float32)
    small[:, P] = P - 1 - j
    small[:, P + 1] = j
    for g, w in enumerate(WINDOWS):
        for e in range(PADW):
            small[:, P + 2 + 16 * g + e] = w / min(w, e + w // 2)
            small[:, P + 2 + 16 * g + 8 + e] = w / min(w, PADW - e + w // 2)
    rows, cs = np.meshgrid(j, j, indexing="ij")
    pos = np.stack([np.maximum(cs - rows, 0), np.maximum(rows - cs, 0), cs + 1, P - cs], axis=1).astype(np.float32)
    pos = np.repeat(pos[:, :, None, :], HEADS, axis=2).reshape(P, 4 * HEADS * P)
    pairs = P // 4
    inv = np.float32(10000.0) ** (-np.arange(pairs, dtype=np.float32) / np.float32(pairs))
    t = np.arange(SAMPLE)
    ang = np.concatenate([np.float32(t // GRID_W)[:, None] * inv, np.float32(t % GRID_W)[:, None] * inv], axis=1).T
    ang = ang.astype(np.float32)
    cos, sin = np.cos(ang), np.sin(ang)
    rope = np.stack([np.concatenate([cos, cos]), np.concatenate([-sin, sin])], axis=1).astype(np.float32)
    return {"small_const": small, "pos_const": pos, "rope_const": rope}


def kernel(**inputs):
    from contextlib import ExitStack
    import concourse.bacc as _bacc
    from concourse.bass_utils import run_bass_kernel_spmd as _run

    nc = _bacc.Bacc("TRN2", target_bir_lowering=False, num_devices=1, dynamic_dma_scratch_size=1024)
    arrays, args = {}, []
    for name, a in [(n, inputs[n]) for n in _INS] + list(constants().items()):
        a = np.ascontiguousarray(a)
        arrays[f"in_{name}_dram"] = a
        args.append(nc.dram_tensor(f"in_{name}_dram", a.shape, mybir.dt.from_np(a.dtype), kind="ExternalInput").ap())
    for i, (shape, dtype) in enumerate(_OUTS):
        args.append(nc.dram_tensor(f"out_{i}_dram", shape, mybir.dt.from_np(np.dtype(dtype)), kind="ExternalOutput").ap())
    with ExitStack() as ctx:
        build(nc, ctx, *args)
    r = _run(nc, [arrays], core_ids=[0])
    return tuple(r.results[0][f"out_{i}_dram"] for i in range(len(_OUTS)))
```
